# Optimizing a Trainium2 kernel written in Bass

```python
import jax, jax.numpy as jnp
from jax import lax
import numpy as np

D_MODEL = 1024
BATCH = 1
SEQ = 256
DEPTH = 2

MEM_LEN = 256
CONV_DIM = 512
CONV_WIDTH = 3
MLA_HEADS = 8
QK_NOPE_DIM = 64
QK_ROPE_DIM = 32
V_HEAD_DIM = 64
Q_RANK = 384
KV_RANK = 256
ROPE_BASE = 10000.0
Q_BLOCK = 128
XATTN_HEADS = 4
XATTN_HEAD_DIM = D_MODEL // XATTN_HEADS
N_EXPERTS = 64
TOP_K = 8
N_GROUPS = 8
TOPK_GROUPS = 4
EXPERT_DIM = 256
SHARED_DIM = 256
ROUTE_SCALE = 2.5
LN_EPS = 1e-5
RMS_EPS = 1e-6
DEEPNORM_ALPHA = (2 * DEPTH) ** 0.25
DEEPNORM_BETA = (8 * DEPTH) ** -0.25
IN_SPLIT_SIZES = (CONV_DIM, CONV_DIM, CONV_DIM, Q_RANK, KV_RANK, QK_ROPE_DIM, D_MODEL, D_MODEL)
IN_DIM = 3 * CONV_DIM + Q_RANK + KV_RANK + QK_ROPE_DIM + 2 * D_MODEL

kernel_name = 'hybrid_conv_mla_memxattn_moe_deepnorm'

def _split_points(sizes):
    pts, acc = [], 0
    for s in sizes[:-1]:
        acc += s
        pts.append(acc)
    return pts

def layer_norm(x, g, b):
    xf = x.astype(jnp.float32)
    mu = jnp.mean(xf, axis=-1, keepdims=True)
    var = jnp.mean(jnp.square(xf - mu), axis=-1, keepdims=True)
    return ((xf - mu) * lax.rsqrt(var + LN_EPS) * g.astype(jnp.float32) + b.astype(jnp.float32)).astype(x.dtype)

def rms_norm(x, g):
    xf = x.astype(jnp.float32)
    ms = jnp.mean(jnp.square(xf), axis=-1, keepdims=True)
    return (xf * lax.rsqrt(ms + RMS_EPS) * g.astype(jnp.float32)).astype(x.dtype)

def rope_tables(positions):
    half = QK_ROPE_DIM // 2
    inv_freq = ROPE_BASE ** (-jnp.arange(half, dtype=jnp.float32) / half)
    ang = positions.astype(jnp.float32)[..., None] * inv_freq
    return jnp.cos(ang), jnp.sin(ang)

def apply_rope(x, cos, sin):
    x1, x2 = jnp.split(x.astype(jnp.float32), 2, axis=-1)
    return jnp.concatenate([x1 * cos - x2 * sin, x2 * cos + x1 * sin], axis=-1).astype(x.dtype)

def short_conv_branch(b_gate, c_gate, h, w_conv, w_conv_out):
    u = c_gate * h
    z = lax.conv_general_dilated(u, w_conv.astype(u.dtype), window_strides=(1,),
                                 padding=[(CONV_WIDTH - 1, 0)],
                                 dimension_numbers=('NWC', 'WIO', 'NWC'),
                                 feature_group_count=CONV_DIM)
    return (b_gate * z) @ w_conv_out

def mla_branch(c_q, c_kv, k_rope, cos, sin, q_norm, w_uq, kv_norm, w_uk, w_uv, w_attn_out):
    bn, s_len, _ = c_q.shape
    q = (rms_norm(c_q, q_norm) @ w_uq).reshape(bn, s_len, MLA_HEADS, QK_NOPE_DIM + QK_ROPE_DIM)
    q_nope = q[..., :QK_NOPE_DIM]
    q_rope = apply_rope(q[..., QK_NOPE_DIM:], cos[:, :, None, :], sin[:, :, None, :])
    ckv = rms_norm(c_kv, kv_norm)
    k_nope = (ckv @ w_uk).reshape(bn, s_len, MLA_HEADS, QK_NOPE_DIM)
    v = (ckv @ w_uv).reshape(bn, s_len, MLA_HEADS, V_HEAD_DIM)
    k_rope = apply_rope(k_rope, cos, sin)
    scale = (QK_NOPE_DIM + QK_ROPE_DIM) ** -0.5
    n_blk = s_len // Q_BLOCK
    qn_blk = q_nope.reshape(bn, n_blk, Q_BLOCK, MLA_HEADS, QK_NOPE_DIM).transpose(1, 0, 2, 3, 4)
    qr_blk = q_rope.reshape(bn, n_blk, Q_BLOCK, MLA_HEADS, QK_ROPE_DIM).transpose(1, 0, 2, 3, 4)
    k_pos = jnp.arange(s_len)

    def attend(args):
        qn, qr, blk = args
        sc = (jnp.einsum('bqhd,bkhd->bhqk', qn, k_nope)
              + jnp.einsum('bqhr,bkr->bhqk', qr, k_rope)).astype(jnp.float32) * scale
        q_pos = blk * Q_BLOCK + jnp.arange(Q_BLOCK)
        sc = jnp.where(k_pos[None, :] <= q_pos[:, None], sc, -jnp.inf)
        p = jax.nn.softmax(sc, axis=-1).astype(v.dtype)
        return jnp.einsum('bhqk,bkhd->bqhd', p, v)

    o = lax.map(attend, (qn_blk, qr_blk, jnp.arange(n_blk)))
    o = o.transpose(1, 0, 2, 3, 4).reshape(bn, s_len, MLA_HEADS * V_HEAD_DIM)
    return o @ w_attn_out

def parallel_mixer(x, cos, sin, w_in, w_conv, w_conv_out, q_norm, w_uq, kv_norm, w_uk, w_uv,
                   w_attn_out, w_mix_out):
    proj = x @ w_in
    b_gate, c_gate, h, c_q, c_kv, k_rope, g_a, g_b = jnp.split(proj, _split_points(IN_SPLIT_SIZES), axis=-1)
    y_a = short_conv_branch(b_gate, c_gate, h, w_conv, w_conv_out)
    y_b = mla_branch(c_q, c_kv, k_rope, cos, sin, q_norm, w_uq, kv_norm, w_uk, w_uv, w_attn_out)
    y = jax.nn.sigmoid(g_a) * y_a + jax.nn.sigmoid(g_b) * y_b
    return y @ w_mix_out

def memory_cross_attention(x, mem, w_xq, w_xk, w_xv, w_xo):
    bn, s_len, _ = x.shape
    m_len = mem.shape[1]
    q = (x @ w_xq).reshape(bn, s_len, XATTN_HEADS, XATTN_HEAD_DIM)
    k = (mem @ w_xk).reshape(bn, m_len, XATTN_HEADS, XATTN_HEAD_DIM)
    v = (mem @ w_xv).reshape(bn, m_len, XATTN_HEADS, XATTN_HEAD_DIM)
    sc = jnp.einsum('bshd,bmhd->bhsm', q, k).astype(jnp.float32) * (XATTN_HEAD_DIM ** -0.5)
    p = jax.nn.softmax(sc, axis=-1).astype(v.dtype)
    o = jnp.einsum('bhsm,bmhd->bshd', p, v).reshape(bn, s_len, D_MODEL)
    return o @ w_xo

def route(x2, w_router, router_bias):
    t = x2.shape[0]
    scores = jax.nn.sigmoid((x2 @ w_router).astype(jnp.float32))
    sel = scores + router_bias.astype(jnp.float32)
    grouped = sel.reshape(t, N_GROUPS, N_EXPERTS // N_GROUPS)
    group_score = jnp.sum(lax.top_k(grouped, 2)[0], axis=-1)
    _, top_groups = lax.top_k(group_score, TOPK_GROUPS)
    group_mask = jnp.sum(jax.nn.one_hot(top_groups, N_GROUPS, dtype=jnp.float32), axis=-2) > 0
    expert_mask = jnp.repeat(group_mask, N_EXPERTS // N_GROUPS, axis=-1)
    _, idx = lax.top_k(jnp.where(expert_mask, sel, -jnp.inf), TOP_K)
    w = jnp.take_along_axis(scores, idx, axis=-1)
    w = w / jnp.sum(w, axis=-1, keepdims=True) * ROUTE_SCALE
    return jnp.sum(jax.nn.one_hot(idx, N_EXPERTS, dtype=jnp.float32) * w[..., None], axis=-2)

def moe_ffn(x, w_router, router_bias, w_gate, w_up, w_down, ws_gate, ws_up, ws_down):
    bn, s_len, d = x.shape
    gates = route(x.reshape(-1, d), w_router, router_bias).reshape(bn, s_len, N_EXPERTS).astype(x.dtype)
    n_blk = s_len // Q_BLOCK
    xb = x.reshape(bn, n_blk, Q_BLOCK, d).transpose(1, 0, 2, 3)
    gb = gates.reshape(bn, n_blk, Q_BLOCK, N_EXPERTS).transpose(1, 0, 2, 3)

    def experts(args):
        xt, gt = args
        hid = jax.nn.silu(jnp.einsum('btd,edf->btef', xt, w_gate)) * jnp.einsum('btd,edf->btef', xt, w_up)
        return jnp.einsum('btef,efd->btd', hid * gt[..., None], w_down)

    routed = lax.map(experts, (xb, gb)).transpose(1, 0, 2, 3).reshape(bn, s_len, d)
    shared = (jax.nn.silu(x @ ws_gate) * (x @ ws_up)) @ ws_down
    return routed + shared

def _normal(key, shape, fan_in, scale=1.0):
    return jax.random.normal(key, shape, jnp.float32) * (scale * fan_in ** -0.5)

def setup_inputs(seed: int = 0) -> dict:
    key = jax.random.key(seed)
    ks = iter(jax.random.split(key, 48))
    L, D = DEPTH, D_MODEL
    beta = DEEPNORM_BETA
    gain = lambda k, n: 1.0 + 0.05 * jax.random.normal(k, (L, n), jnp.float32)
    bias = lambda k, n: 0.02 * jax.random.normal(k, (L, n), jnp.float32)
    x = jax.random.normal(next(ks), (BATCH, SEQ, D), jnp.float32)
    mem = jax.random.normal(next(ks), (BATCH, MEM_LEN, D), jnp.float32)
    offsets = jax.random.randint(next(ks), (BATCH, 1), 0, 4096, dtype=jnp.int32)
    positions = offsets + jnp.arange(SEQ, dtype=jnp.int32)[None, :]
    return {
        'x': x,
        'mem': mem,
        'positions': positions,
        'w_in': _normal(next(ks), (L, D, IN_DIM), D),
        'w_conv': _normal(next(ks), (L, CONV_WIDTH, 1, CONV_DIM), CONV_WIDTH),
        'w_conv_out': _normal(next(ks), (L, CONV_DIM, D), CONV_DIM, beta),
        'q_norm': gain(next(ks), Q_RANK),
        'w_uq': _normal(next(ks), (L, Q_RANK, MLA_HEADS * (QK_NOPE_DIM + QK_ROPE_DIM)), Q_RANK),
        'kv_norm': gain(next(ks), KV_RANK),
        'w_uk': _normal(next(ks), (L, KV_RANK, MLA_HEADS * QK_NOPE_DIM), KV_RANK),
        'w_uv': _normal(next(ks), (L, KV_RANK, MLA_HEADS * V_HEAD_DIM), KV_RANK, beta),
        'w_attn_out': _normal(next(ks), (L, MLA_HEADS * V_HEAD_DIM, D), MLA_HEADS * V_HEAD_DIM, beta),
        'w_mix_out': _normal(next(ks), (L, D, D), D, beta),
        'ln1_g': gain(next(ks), D),
        'ln1_b': bias(next(ks), D),
        'w_xq': _normal(next(ks), (L, D, D), D),
        'w_xk': _normal(next(ks), (L, D, D), D),
        'w_xv': _normal(next(ks), (L, D, D), D, beta),
        'w_xo': _normal(next(ks), (L, D, D), D, beta),
        'ln2_g': gain(next(ks), D),
        'ln2_b': bias(next(ks), D),
        'w_router': _normal(next(ks), (L, D, N_EXPERTS), D),
        'router_bias': 0.01 * jax.random.normal(next(ks), (L, N_EXPERTS), jnp.float32),
        'w_gate': _normal(next(ks), (L, N_EXPERTS, D, EXPERT_DIM), D),
        'w_up': _normal(next(ks), (L, N_EXPERTS, D, EXPERT_DIM), D),
        'w_down': _normal(next(ks), (L, N_EXPERTS, EXPERT_DIM, D), EXPERT_DIM, beta),
        'ws_gate': _normal(next(ks), (L, D, SHARED_DIM), D),
        'ws_up': _normal(next(ks), (L, D, SHARED_DIM), D),
        'ws_down': _normal(next(ks), (L, SHARED_DIM, D), SHARED_DIM, beta),
        'ln3_g': gain(next(ks), D),
        'ln3_b': bias(next(ks), D),
    }

def reference(x, mem, positions, w_in, w_conv, w_conv_out, q_norm, w_uq, kv_norm, w_uk, w_uv,
              w_attn_out, w_mix_out, ln1_g, ln1_b, w_xq, w_xk, w_xv, w_xo, ln2_g, ln2_b,
              w_router, router_bias, w_gate, w_up, w_down, ws_gate, ws_up, ws_down, ln3_g, ln3_b):
    cos, sin = rope_tables(positions)
    for l in range(DEPTH):
        mix = parallel_mixer(x, cos, sin, w_in[l], w_conv[l], w_conv_out[l], q_norm[l], w_uq[l],
                             kv_norm[l], w_uk[l], w_uv[l], w_attn_out[l], w_mix_out[l])
        x = layer_norm(DEEPNORM_ALPHA * x + mix, ln1_g[l], ln1_b[l])
        xat = memory_cross_attention(x, mem, w_xq[l], w_xk[l], w_xv[l], w_xo[l])
        x = layer_norm(DEEPNORM_ALPHA * x + xat, ln2_g[l], ln2_b[l])
        ffn = moe_ffn(x, w_router[l], router_bias[l], w_gate[l], w_up[l], w_down[l],
                      ws_gate[l], ws_up[l], ws_down[l])
        x = layer_norm(DEEPNORM_ALPHA * x + ffn, ln3_g[l], ln3_b[l])
    return x


_drawn_inputs = setup_inputs


def setup_inputs(seed=0):
    import zlib

    import numpy as np

    out = dict(_drawn_inputs(seed))
    spreads = {}
    factors = {'q_norm': 7.975, 'kv_norm': 5.383}
    for name, (base, spread) in spreads.items():
        noise = np.random.default_rng([zlib.crc32(name.encode()), seed]).standard_normal(out[name].shape)
        drawn = base * np.exp(spread * noise) if base else spread * noise
        out[name] = __import__('jax').numpy.asarray(drawn.astype(out[name].dtype))
    for name, factor in factors.items():
        out[name] = (out[name] * factor).astype(out[name].dtype)
    return out
```

```python
from contextlib import ExitStack

import numpy as np

import concourse.bass as bass
from concourse import mybir

ALU = mybir.AluOpType
ACT = mybir.ActivationFunctionType
AX_X = mybir.AxisListType.X
F32 = mybir.dt.float32
F32R = mybir.dt.float32r
I32 = mybir.dt.int32

P = 128
D_MODEL = 1024
SEQ = 256
DEPTH = 2
MEM_LEN = 256
CONV_DIM = 512
CONV_WIDTH = 3
HEADS = 8
NOPE = 64
ROPE = 32
HALF_ROPE = ROPE // 2
QK = NOPE + ROPE
V_DIM = 64
Q_RANK = 384
KV_RANK = 256
ROPE_BASE = 10000.0
X_HEADS = 4
X_DIM = D_MODEL // X_HEADS
EXPERTS = 64
TOP_K = 8
GROUPS = 8
TOP_GROUPS = 4
EXPERT_DIM = 256
ROUTE_SCALE = 2.5
LN_EPS = 1e-5
RMS_EPS = 1e-6
ALPHA = (2 * DEPTH) ** 0.25
MLA_SCALE = QK ** -0.5
X_SCALE = X_DIM ** -0.5

TT = SEQ // P
KC = D_MODEL // P
BANK = 512
SLOT = KC * BANK
RING = 6
SLOTS = 64
PAIRS = EXPERTS // 2
BODIES = PAIRS // 2
PADDED = EXPERTS + 4
MASKED = -1e30
FAR = 1e4
TAKEN = 3e30

IN_B, IN_C, IN_H = 0, CONV_DIM, 2 * CONV_DIM
IN_Q = 3 * CONV_DIM
IN_KV = IN_Q + Q_RANK
IN_GA = IN_KV + KV_RANK + ROPE
IN_GB = IN_GA + D_MODEL

STAGES = [
    ("cq", 2), ("ckv", 2), ("c", 2), ("h", 2), ("b", 2), ("rankT", 3), ("uq", 4), ("uk", 2), ("uv", 2),
    ("ga0", 2), ("qkT", 8), ("scores", 8), ("ga1", 2), ("gb", 4), ("pT", 8), ("oT", 2),
    ("ya", 4), ("yb", 4), ("mix", 4), ("xk", 4), ("xT1", 4), ("xq", 4), ("xscores", 4), ("xv", 4),
    ("xpT", 4), ("xoT", 4), ("xo", 4), ("xT2", 4), ("router", 1), ("shared", 2), ("place", 1), ("xT3", 4),
]
WORK = 4
FIRST_JOB, n_jobs = {}, 0
for _name, _count in STAGES:
    FIRST_JOB[_name] = n_jobs
    n_jobs += _count
JOBS = dict(STAGES)
SETUP_USES = 2
BANK_USES = [len(range(b, n_jobs, WORK)) for b in range(WORK)]


def job(stage, i=0):
    assert i < JOBS[stage]
    n = FIRST_JOB[stage] + i
    return n % WORK, SETUP_USES + n // WORK + 1


LOADS = ["cq", "ckv_uv", "c", "h", "b", "uq_uk", "ga0", "ga1", "gb0", "gb1", "conv_out", "attn_out",
         "mix0", "mix1", "xk0", "xk1", "xq0", "xq1", "xv0", "xv1", "xo0", "xo1", "shared", "down_router"]
DENSE_USES = len(LOADS) // RING
assert len(LOADS) % RING == 0

PAR_Q = 0
PAR_KV = PAR_Q + Q_RANK // P
PAR_CONV = PAR_KV + KV_RANK // P
PAR_LN = PAR_CONV + CONV_WIDTH * (CONV_DIM // P)
PAR_BIAS = PAR_LN + 6 * KC
N_PAR = PAR_BIAS + EXPERTS


def build_trunk(nc, x, mem, positions, w_in, w_conv, w_conv_out, q_norm, w_uq, kv_norm, w_uk, w_uv,
                w_attn_out, w_mix_out, ln1_g, ln1_b, w_xq, w_xk, w_xv, w_xo, ln2_g, ln2_b,
                w_router, router_bias, w_gate, w_up, w_down, ws_gate, ws_up, ws_down, ln3_g, ln3_b, out):
    with ExitStack() as ctx:
        def sb(name, shape, dt=F32):
            return ctx.enter_context(nc.sbuf_tensor(name, shape, dt))

        def sem(name):
            return ctx.enter_context(nc.semaphore(name))

        ring = sb("ring", [P, RING, SLOT])
        X = sb("X", [P, TT, D_MODEL])
        XT = sb("XT", [P, KC, SEQ])
        memT = sb("memT", [P, KC, MEM_LEN])
        arena = sb("arena", [P, 18 * 1024])
        out_hi = sb("out_hi", [P, D_MODEL], F32R)
        out_lo = sb("out_lo", [P, D_MODEL], F32R)
        selT = sb("selT", [P, 2, SEQ], F32R)
        ident = sb("ident", [P, P])
        earlier = sb("earlier", [P, P])
        mask = sb("mask", [P, 3 * P])
        iota = sb("iota", [P, SLOTS])
        par_all = sb("par_all", [P, DEPTH, N_PAR])
        par = sb("par", [P, N_PAR])
        cos = sb("cos", [P, TT, HALF_ROPE])
        sin = sb("sin", [P, TT, HALF_ROPE])
        small = sb("small", [P, 96])
        rounds = sb("rounds", [1, DEPTH], I32)
        bodies = sb("bodies", [1, DEPTH + 1], I32)

        def view(at, *shape):
            n = int(np.prod(shape))
            v = arena[:, at:at + n]
            if len(shape) == 2:
                return v.rearrange("p (a b) -> p a b", a=shape[0])
            if len(shape) == 3:
                return v.rearrange("p (a b c) -> p a b c", a=shape[0], b=shape[1])
            return v

        K = 1024
        gb = view(0, 2, D_MODEL)
        XN = view(16 * K, TT, D_MODEL)
        pT = view(0, HEADS, 3 * P)
        cqn = view(0, TT, Q_RANK)
        ckvn = view(768, TT, KV_RANK)
        cqT = view(1280, Q_RANK // P, SEQ)
        ckvT = view(2048, KV_RANK // P, SEQ)
        kr = view(2560, TT, ROPE)
        c_sb = view(2 * K + 640, CONV_DIM // P, SEQ)
        u_pad = view(3 * K + 640, CONV_DIM // P, SEQ + 2)
        b_sb = view(4 * K + 704, CONV_DIM // P, SEQ)
        sgB = view(3 * K, KC, SEQ)
        q_cat = view(6 * K, TT, HEADS, QK)
        k_cat = view(6 * K + 1536, TT, HEADS, QK)
        S = view(6 * K, HEADS, 3 * P)
        yT = view(6 * K, KC, SEQ)
        qT = view(9 * K, HEADS, SEQ)
        kT = view(11 * K, HEADS, SEQ)
        V = view(13 * K, TT, HEADS * V_DIM)
        z = view(14 * K, CONV_DIM // P, SEQ)
        oT = view(15 * K, HEADS // 2, SEQ)
        sgA = view(16 * K, KC, SEQ)
        rope_t = view(11 * K, 4, TT * HEADS * HALF_ROPE)
        xkT = view(2 * K, KC, MEM_LEN)
        xV = view(4 * K, TT, D_MODEL)
        xqT = view(6 * K, KC, SEQ)
        xS = view(8 * K, X_HEADS, TT * MEM_LEN)
        xpT = view(10 * K, X_HEADS, 2, SEQ)
        xoT = view(12 * K, KC, SEQ)
        xg = [view(2 * K + b * K, KC, P) for b in range(2)]
        sel = [view(4 * K + b * 256, TT, P) for b in range(2)]
        act_gate = view(5 * K - 512, EXPERT_DIM)
        hid = view(5 * K - 256, EXPERT_DIM)
        hidT = view(5 * K, 2, P)
        sharedT = view(5 * K + 256, 2, SEQ)
        shared_act = view(6 * K, 2, SEQ)
        score = view(6 * K + 512, TT, EXPERTS)
        biased = view(6 * K + 640, TT, EXPERTS)
        masked = view(6 * K + 768, TT, EXPERTS)
        marked = view(6 * K + 896, TT, EXPERTS)
        chosen = view(7 * K, TT, EXPERTS)
        weight = view(7 * K + 128, TT, EXPERTS)
        gates = view(7 * K + 256, TT, PADDED)
        pos = view(7 * K + 256 + 2 * PADDED, TT, PADDED)
        top2 = view(7 * K + 768, TT * GROUPS, 8)
        cmp_a = view(8 * K, TT * GROUPS, GROUPS)
        cmp_b = view(8 * K + 128, TT * GROUPS, GROUPS)
        before_group = view(8 * K + 256, GROUPS, GROUPS)
        ones = view(8 * K + 640, P)
        gpair = [view(8 * K + 768 + 4 * b, TT, 2) for b in range(2)]
        mem_sb = view(0, TT, D_MODEL)
        ang = view(2 * K, 8, TT * HALF_ROPE)
        pos_i = sb("pos_i", [P, TT], I32)
        pos_f = small[:, 0:2]
        sumsq = small[:, 2:6]
        rstd = small[:, 6:10]
        row_max = small[:, 10:26].rearrange("p (h t) -> p h t", t=TT)
        row_sum = small[:, 26:42].rearrange("p (h t) -> p h t", t=TT)
        moments = small[:, 54:58]
        ln_rstd = small[:, 90:92]
        group_score = small[:, 58:74]
        group_rank = small[:, 74:90]
        top8 = sb("top8", [P, TT, 8])
        gate_sum = sb("gate_sum", [P, TT])
        slot_gate = sb("slot_gate", [P, 2])
        busiest = sb("busiest", [P, 4])
        bodies_f = sb("bodies_f", [1, 2])
        penalty = sb("penalty", [P, TT * GROUPS])
        stats = sb("stats", [P, TT, 12])
        minus_half = sb("minus_half", [P, 1])
        inv_freq = sb("inv_freq", [P, HALF_ROPE])

        work = [ctx.enter_context(nc.psum_tensor(f"work{b}", [P, BANK], F32)) for b in range(WORK)]
        moe_sum = [ctx.enter_context(nc.psum_tensor(f"moe_sum{b}", [P, BANK], F32)) for b in range(4)]

        passed = sem("passed")
        x_loaded = sem("x_loaded")
        mem_loaded = sem("mem_loaded")
        small_loaded = sem("small_loaded")
        consts_ready = sem("consts_ready")
        angles_ready = sem("angles_ready")
        sines_ready = sem("sines_ready")
        rope_ready = sem("rope_ready")
        slot_loaded = [sem(f"slot_loaded{s}") for s in range(RING)]
        filled = [sem(f"filled{b}") for b in range(WORK)]
        taken = [sem(f"taken{b}") for b in range(WORK)]
        act_order = sem("act_order")
        dve_order = sem("dve_order")
        pool_order = sem("pool_order")
        squares_ready = sem("squares_ready")
        qk_ready = sem("qk_ready")
        conv_ready = sem("conv_ready")
        max_ready = sem("max_ready")
        exp_ready = sem("exp_ready")
        probs_ready = sem("probs_ready")
        y_ready = sem("y_ready")
        rstd_ready = sem("rstd_ready")
        moments_ready = sem("moments_ready")
        ln_rstd_ready = sem("ln_rstd_ready")
        norm_ready = sem("norm_ready")
        ln_loaded = sem("ln_loaded")
        ln_applied = sem("ln_applied")
        xmax_ready = sem("xmax_ready")
        xprobs_ready = sem("xprobs_ready")
        chosen_ready = sem("chosen_ready")
        routing_ready = sem("routing_ready")
        shared_down = sem("shared_down")
        sel_ready = sem("sel_ready")
        gate_up_done = sem("gate_up_done")
        silu_ready = sem("silu_ready")
        hid_ready = sem("hid_ready")
        selT_filled = sem("selT_filled")
        selT_ready = sem("selT_ready")
        hidT_filled = sem("hidT_filled")
        hidT_ready = sem("hidT_ready")
        gather_filled = [sem("gather_filled_a"), sem("gather_filled_b")]
        gather_ready = [sem("gather_ready_a"), sem("gather_ready_b")]
        down_filled = [sem("down_filled_0"), sem("down_filled_1")]
        hi_ready = [sem("hi_ready_0"), sem("hi_ready_1")]
        lo_ready = [sem("lo_ready_0"), sem("lo_ready_1")]
        scattered = sem("scattered")
        out_stored = sem("out_stored")

        def alone(eng, s, value):
            eng.wait_ge(s, value)
            eng.sem_inc(passed, 1)

        def ordered(eng, s):
            n, last = [0], [None]

            def step(ins):
                n[0] += 1
                last[0] = (s, n[0])
                return ins.then_inc(s, 1)

            def tell(ins, semaphore, value):
                last[0] = (semaphore, value)
                return ins.then_inc(semaphore, 1)

            def take(ins, l, stage, i=0):
                b, k = job(stage, i)
                return tell(ins, taken[b], l * BANK_USES[b] + k)

            def settle():
                if last[0]:
                    eng.wait_ge(*last[0])

            def restart():
                if n[0]:
                    eng.wait_ge(s, n[0])
                    eng.sem_clear(s)
                n[0], last[0] = 0, None

            return step, tell, take, settle, restart

        def wait_filled(eng, l, stage, i=0):
            b, n = job(stage, i)
            eng.wait_ge(filled[b], l * BANK_USES[b] + n)
            return work[b]

        def wait_taken(eng, l, stage, count=None, first=0):
            last = {}
            for i in range(first, JOBS[stage] if count is None else first + count):
                b, n = job(stage, i)
                last[b] = n
            for b, n in last.items():
                eng.wait_ge(taken[b], l * BANK_USES[b] + n)

        def chunks(slot, k, n, at=0):
            return ring[:, slot, at:at + k * n].rearrange("p (k n) -> p k n", k=k)

        block = ctx.enter_context(nc.Block())

        @block.sync
        def _(sp):
            x2, m2 = x.rearrange("o s d -> (o s) d"), mem.rearrange("o s d -> (o s) d")
            sp.dma_start(mem_sb, m2.rearrange("(t p) d -> p t d", p=P)).then_inc(mem_loaded, 16)
            sp.dma_start(X[:, :, :], x2.rearrange("(t p) d -> p t d", p=P)).then_inc(x_loaded, 16)
            sp.wait_ge(consts_ready, 1)

            by_feature = {"cq": (IN_Q, Q_RANK), "c": (IN_C, BANK), "h": (IN_H, BANK), "b": (IN_B, BANK),
                          "ga0": (IN_GA, BANK), "ga1": (IN_GA + BANK, BANK),
                          "gb0": (IN_GB, BANK), "gb1": (IN_GB + BANK, BANK)}
            square = {"xk": w_xk, "xq": w_xq, "xv": w_xv}

            def layer_of(w, l):
                return w[bass.ds(l, 1)].rearrange("o k n -> (o k) n")

            def sources(name, l, s):
                if name in by_feature or name[:-1] in square:
                    if name in by_feature:
                        at, n = by_feature[name]
                        w = layer_of(w_in, l)
                    else:
                        at, n = BANK * int(name[-1]), BANK
                        w = layer_of(square[name[:-1]], l)
                    v = w[:, at:at + n].rearrange("(p k) n -> p k n", k=KC)
                    dst = chunks(s, KC, n)
                    return [(dst[:, 0:4], v[:, 0:4]), (dst[:, 4:8], v[:, 4:8])]
                if name == "ckv_uv":
                    n = KV_RANK + ROPE
                    return [(chunks(s, KC, n), layer_of(w_in, l)[:, IN_KV:IN_KV + n].rearrange("(p k) n -> p k n", k=KC)),
                            (chunks(s, 2, 512, KC * n), layer_of(w_uv, l).rearrange("(k p) n -> p k n", p=P))]
                if name == "uq_uk":
                    n = HEADS * QK
                    return [(chunks(s, 3, n), layer_of(w_uq, l).rearrange("(k p) n -> p k n", p=P)),
                            (chunks(s, 2, 512, 3 * n), layer_of(w_uk, l).rearrange("(k p) n -> p k n", p=P))]
                if name in ("conv_out", "attn_out"):
                    w = layer_of(w_conv_out if name == "conv_out" else w_attn_out, l)
                    v = w.rearrange("(k p) n -> p k n", p=P)
                    dst = chunks(s, 4, D_MODEL)
                    return [(dst[:, 0:2], v[:, 0:2]), (dst[:, 2:4], v[:, 2:4])]
                if name in ("mix0", "mix1", "xo0", "xo1"):
                    at = BANK * int(name[-1])
                    w = layer_of(w_mix_out if name[:3] == "mix" else w_xo, l)
                    v = w[:, at:at + BANK].rearrange("(k p) n -> p k n", p=P)
                    dst = chunks(s, KC, BANK)
                    return [(dst[:, 0:4], v[:, 0:4]), (dst[:, 4:8], v[:, 4:8])]
                if name == "shared":
                    return [(chunks(s, KC, EXPERT_DIM), layer_of(ws_gate, l).rearrange("(p k) n -> p k n", k=KC)),
                            (chunks(s, KC, EXPERT_DIM, SLOT // 2), layer_of(ws_up, l).rearrange("(p k) n -> p k n", k=KC))]
                assert name == "down_router"
                return [(chunks(s, 2, D_MODEL), layer_of(ws_down, l).rearrange("(k p) n -> p k n", p=P)),
                        (chunks(s, KC, EXPERTS, 2 * D_MODEL), layer_of(w_router, l).rearrange("(p k) n -> p k n", k=KC))]

            last_job = {"cq": ("cq", 1), "ckv_uv": ("uv", 1), "c": ("c", 1), "h": ("h", 1), "b": ("b", 1),
                        "uq_uk": ("uk", 1), "ga0": ("ga0", 1), "ga1": ("ga1", 1), "gb0": ("gb", 1), "gb1": ("gb", 3),
                        "conv_out": ("ya", 3), "attn_out": ("yb", 3), "shared": ("shared", 1)}
            for stage in ("mix", "xk", "xq", "xv", "xo"):
                last_job[stage + "0"], last_job[stage + "1"] = (stage, 1), (stage, 3)

            def wait_read(l, n):
                if LOADS[n] == "down_router":
                    alone(sp, shared_down, l + 1)
                else:
                    b, k = job(*last_job[LOADS[n]])
                    alone(sp, filled[b], l * BANK_USES[b] + k)

            def load_ln(l, g, b, which):
                sp.wait_ge(ln_applied, l * 3 + which + 1)
                for j, w in ((0, g), (1, b)):
                    sp.dma_start(gb[:, j, :], w[bass.ds(l, 1)].rearrange("o d -> (o d)").partition_broadcast(P)
                                 ).then_inc(ln_loaded, 16)

            e_gate = w_gate.rearrange("l e (p k) f -> (l e) p k f", k=KC)
            e_up = w_up.rearrange("l e (p k) f -> (l e) p k f", k=KC)
            e_down = w_down.rearrange("l e (k p) d -> (l e) p k d", p=P)
            more, start = sp.alloc_register("sp_rounds"), sp.alloc_register("sp_start")
            with sp.Fori(0, DEPTH) as l:
                base = sp.value_load(bodies[0:1, bass.ds(l, 1)], min_val=0, max_val=4 * BODIES * DEPTH)
                for n, name in enumerate(LOADS):
                    s = n % RING
                    if n < RING:
                        alone(sp, down_filled[1] if s % 3 == 2 else gate_up_done, base * 2 + 1)
                    else:
                        wait_read(l, n - RING)
                    if name == "xq1":
                        load_ln(l, ln1_g, ln1_b, 0)
                    for dst, src in sources(name, l, s):
                        sp.dma_start(dst, src).then_inc(slot_loaded[s], 16)
                load_ln(l, ln2_g, ln2_b, 1)

                def load_experts(l, i, free):
                    first = sp.snap(l * EXPERTS + i * 4)
                    for j in range(2):
                        for e in range(2):
                            s = 3 * j + e
                            free(j, s)
                            at = bass.ds(first + (2 * j + e), 1)
                            for h, w in enumerate((e_gate, e_up)):
                                sp.dma_start(chunks(s, KC, EXPERT_DIM, h * SLOT // 2),
                                             w[at].rearrange("o p k f -> (o p) k f")).then_inc(slot_loaded[s], 16)
                        s = 3 * j + 2
                        free(j, s)
                        for e in range(2):
                            at = bass.ds(first + (2 * j + e), 1)
                            sp.dma_start(chunks(s, 2, D_MODEL, e * SLOT // 2),
                                         e_down[at].rearrange("o p k d -> (o p) k d")).then_inc(slot_loaded[s], 16)

                load_experts(l, 0, lambda j, s: wait_read(l, len(LOADS) - RING + s))
                sp.reg_mov(more, 1)
                sp.reg_mov(start, 1)
                with sp.Fori(0, more) as r:
                    with sp.Fori(start, BODIES) as i:
                        gathers = sp.snap((base + r * BODIES + i) * 2 + l)
                        load_experts(l, i, lambda j, s: sp.wait_ge(gather_filled[1] if s % 3 == 2 else selT_filled,
                                                                   gathers + j))
                    sp.reg_mov(start, 0)
                    alone(sp, routing_ready, l + 1)
                    sp.reg_load(more, rounds[0:1, bass.ds(l, 1)])
                load_ln(l, ln3_g, ln3_b, 2)
            sp.wait_ge(ln_applied, 3 * DEPTH + 1)
            sp.dma_start(out.rearrange("o (t p) d -> p (o t) d", p=P), X[:, :, :]).then_inc(out_stored, 16)
            sp.wait_ge(out_stored, 16)

        @block.gpsimd
        def _(pool):
            step, tell, take, settle, restart = ordered(pool, pool_order)
            tell(pool.memset(bodies[:, :], 0), consts_ready, 1)
            pool.dma_start(pos_i[:, :], positions.rearrange("o (t p) -> p (o t)", p=P),
                           allow_slow_non_contiguous=True).then_inc(small_loaded, 16)
            for at, w in ((PAR_Q, q_norm), (PAR_KV, kv_norm),
                               (PAR_CONV, w_conv.rearrange("l w o d -> l (w o d)"))):
                v = w.rearrange("l (c p) -> l p c", p=P)
                for n in range(DEPTH):
                    pool.dma_start(par_all[:, n, at:at + v.shape[2]], v[n],
                                   allow_slow_non_contiguous=True).then_inc(small_loaded, 16)
            for j, w in enumerate((ln1_g, ln1_b, ln2_g, ln2_b, ln3_g, ln3_b)):
                pool.dma_start(par_all[:, :, PAR_LN + j * KC:PAR_LN + (j + 1) * KC],
                               w.rearrange("l (p k) -> p l k", k=KC)).then_inc(small_loaded, 16)
            pool.dma_start(par_all[:, :, PAR_BIAS:], router_bias.partition_broadcast(P)).then_inc(small_loaded, 16)
            step(pool.memset(ident[:, :], 0.0))
            step(pool.memset(earlier[:, :], 0.0))
            step(pool.memset(mask[:, :], 0.0))
            step(pool.memset(minus_half[:, :], -0.5))
            step(pool.iota(iota[:, :], pattern=[[1, SLOTS]], base=0, channel_multiplier=0,
                           allow_small_or_imprecise_dtypes=True))
            for i in range(HALF_ROPE):
                f = float(np.float32(ROPE_BASE) ** np.float32(-i / HALF_ROPE))
                step(pool.memset(inv_freq[:, i:i + 1], f))
            settle()
            step(pool.affine_select(out=ident[:, :], in_=ident[:, :], compare_op=ALU.not_equal, fill=1.0,
                                    base=0, pattern=[[-1, P]], channel_multiplier=1))
            step(pool.affine_select(out=earlier[:, :], in_=earlier[:, :], compare_op=ALU.is_ge, fill=1.0,
                                    base=0, pattern=[[-1, P]], channel_multiplier=1))
            for c in (0, 2):
                m = mask[:, c * P:(c + 1) * P]
                ins = pool.affine_select(out=m, in_=m, compare_op=ALU.is_ge, fill=MASKED,
                                         base=0, pattern=[[-1, P]], channel_multiplier=1)
                if c == 0:
                    step(ins)
                else:
                    tell(ins, consts_ready, 2)
            restart()
            pool.sem_inc(ln_applied, 1)

            def inverse_root(dst, src, eps, ready):
                step(pool.tensor_scalar(dst, src, eps, None, ALU.add))
                settle()
                pool.tensor_tensor(dst, dst, minus_half[:, :], ALU.pow).then_inc(ready, 1)

            with pool.Fori(0, DEPTH) as l:
                for i in range(4):
                    alone(pool, squares_ready, l * 4 + (i + 1))
                    inverse_root(rstd[:, i:i + 1], sumsq[:, i:i + 1], RMS_EPS, rstd_ready)
                for which in range(3):
                    for t in range(TT):
                        alone(pool, moments_ready, l * 6 + (2 * which + t + 1))
                        inverse_root(ln_rstd[:, t:t + 1], moments[:, 2 * t + 1:2 * t + 2], LN_EPS, ln_rstd_ready)
                    pool.wait_ge(norm_ready, l * 6 + 2 * which + 2)
                    pool.wait_ge(ln_loaded, (l * 3 + which + 1) * 32)
                    for t in range(TT):
                        step(pool.tensor_tensor(X[:, t, :], XN[:, t, :], gb[:, 0, :], ALU.mult))
                    settle()
                    for t in range(TT):
                        ins = pool.tensor_tensor(X[:, t, :], X[:, t, :], gb[:, 1, :], ALU.add)
                        if t == 0:
                            step(ins)
                        else:
                            ins.then_inc(ln_applied, 1)
                restart()

        @block.tensor
        def _(pe):
            seen = {}

            def wait_stages(l, *stages):
                last = {}
                for stage in stages:
                    for i in range(JOBS[stage]):
                        b, n = job(stage, i)
                        last[b] = max(n, last.get(b, 0))
                for b, n in last.items():
                    if n > seen.get(b, -1):
                        pe.wait_ge(taken[b], l * BANK_USES[b] + n)
                        seen[b] = n

            def open_job(l, stage, i=0):
                b, n = job(stage, i)
                if n - 1 > seen.get(b, -1):
                    pe.wait_ge(taken[b], l * BANK_USES[b] + (n - 1))
                    seen[b] = n - 1
                return work[b]

            def close_job(mm, stage, i=0):
                mm.then_inc(filled[job(stage, i)[0]], 1)

            def wait_load(uses, name):
                n = LOADS.index(name)
                pe.wait_ge(slot_loaded[n % RING], (uses + (n // RING + 1)) * 32)
                return n % RING

            def accumulate(dst, pairs):
                for k, (a, b) in enumerate(pairs):
                    mm = pe.matmul(dst, a, b, start=(k == 0), stop=(k == len(pairs) - 1))
                return mm

            pe.wait_ge(consts_ready, 2)
            for n, src in enumerate([mem_sb] * 4 + [X] * 4):
                if n == 0:
                    pe.wait_ge(mem_loaded, 16)
                if n == 4:
                    pe.wait_ge(x_loaded, 16)
                if n >= WORK:
                    pe.wait_ge(taken[n % WORK], 1)
                for c in range(2):
                    for t in range(TT):
                        mm = pe.transpose(work[n % WORK][:, (c * TT + t) * P:(c * TT + t + 1) * P],
                                          src[:, t, 2 * (n % 4) + c::KC], ident[:, :])
                mm.then_inc(filled[n % WORK], 1)
            for b in range(WORK):
                pe.wait_ge(taken[b], SETUP_USES)
            pe.sem_inc(gate_up_done, 1)
            pe.sem_inc(down_filled[1], 1)

            def transpose_norm(l, stage, which):
                pe.wait_ge(norm_ready, l * 6 + 2 * which + 2)
                for i in range(4):
                    w = open_job(l, stage, i)
                    for c in range(2):
                        for t in range(TT):
                            mm = pe.transpose(w[:, (c * TT + t) * P:(c * TT + t + 1) * P],
                                              XN[:, t, 2 * i + c::KC], ident[:, :])
                    close_job(mm, stage, i)

            def by_token(l, stage, i, t, src, weights, n, at=0):
                w = open_job(l, stage, i)
                k = weights.shape[1]
                mm = accumulate(w[:, 0:n], [(src[:, c, t * P:(t + 1) * P], weights[:, c, at:at + n]) for c in range(k)])
                close_job(mm, stage, i)

            def by_feature(l, stage, i, src, weights, at=0):
                w = open_job(l, stage, i)
                k = weights.shape[1]
                for m in range(2):
                    cols = slice(at + m * P, at + (m + 1) * P)
                    mm = accumulate(w[:, m * SEQ:(m + 1) * SEQ], [(weights[:, c, cols], src[:, c, :]) for c in range(k)])
                close_job(mm, stage, i)
                return mm

            more = pe.alloc_register("pe_rounds")
            with pe.Fori(0, DEPTH) as l:
                base = pe.value_load(bodies[0:1, bass.ds(l, 1)], min_val=0, max_val=4 * BODIES * DEPTH)
                uses = pe.snap(base + l * DENSE_USES)
                s = wait_load(uses, "cq")
                for t in range(TT):
                    by_token(l, "cq", t, t, XT, chunks(s, KC, Q_RANK), Q_RANK)
                s = wait_load(uses, "ckv_uv")
                for t in range(TT):
                    by_token(l, "ckv", t, t, XT, chunks(s, KC, KV_RANK + ROPE), KV_RANK + ROPE)
                for name in ("c", "h", "b"):
                    s = wait_load(uses, name)
                    for i in range(2):
                        by_feature(l, name, i, XT, chunks(s, KC, BANK), i * 2 * P)
                wait_stages(l, "cq", "ckv")
                for i, blocks in enumerate(([(cqn, 0), (cqn, 1)], [(cqn, 2)], [(ckvn, 0), (ckvn, 1)])):
                    w = open_job(l, "rankT", i)
                    for j, (src, c) in enumerate(blocks):
                        for t in range(TT):
                            mm = pe.transpose(w[:, (j * TT + t) * P:(j * TT + t + 1) * P],
                                              src[:, t, c * P:(c + 1) * P], ident[:, :])
                    close_job(mm, "rankT", i)
                s = wait_load(uses, "uq_uk")
                wait_stages(l, "rankT")
                w_uq_sb = chunks(s, 3, HEADS * QK)
                for i in range(4):
                    by_token(l, "uq", i, i // 2, cqT, w_uq_sb, Q_RANK, (i % 2) * Q_RANK)
                for t in range(TT):
                    by_token(l, "uk", t, t, ckvT, chunks(s, 2, 512, 3 * HEADS * QK), 512)
                s = LOADS.index("ckv_uv") % RING
                for t in range(TT):
                    by_token(l, "uv", t, t, ckvT, chunks(s, 2, 512, KC * (KV_RANK + ROPE)), 512)
                s = wait_load(uses, "ga0")
                for i in range(2):
                    by_feature(l, "ga0", i, XT, chunks(s, KC, BANK), i * 2 * P)
                pe.wait_ge(qk_ready, l + 1)
                for i in range(8):
                    src = (q_cat, k_cat)[i % 2]
                    t, g = i // 2 % 2, i // 4
                    w = open_job(l, "qkT", i)
                    for j in range(4):
                        mm = pe.transpose(w[0:QK, j * P:(j + 1) * P], src[:, t, 4 * g + j, :], ident[:, :])
                    close_job(mm, "qkT", i)
                wait_stages(l, "qkT")
                for h in range(HEADS):
                    w = open_job(l, "scores", h)
                    pe.matmul(w[:, 0:P], qT[0:QK, h, 0:P], kT[0:QK, h, 0:P], start=True, stop=True)
                    mm = pe.matmul(w[:, P:3 * P], qT[0:QK, h, P:SEQ], kT[0:QK, h, :], start=True, stop=True)
                    close_job(mm, "scores", h)
                s = wait_load(uses, "ga1")
                for i in range(2):
                    by_feature(l, "ga1", i, XT, chunks(s, KC, BANK), i * 2 * P)
                for i in range(4):
                    name = f"gb{i // 2}"
                    s = wait_load(uses, name)
                    by_feature(l, "gb", i, XT, chunks(s, KC, BANK), (i % 2) * 2 * P)
                for h in range(HEADS):
                    if h % 4 == 0:
                        pe.wait_ge(probs_ready, l * 2 + (h // 4 + 1))
                    w = open_job(l, "pT", h)
                    for j in range(3):
                        mm = pe.transpose(w[:, j * P:(j + 1) * P], S[:, h, j * P:(j + 1) * P], ident[:, :])
                    close_job(mm, "pT", h)
                wait_stages(l, "pT", "uv")
                for i in range(2):
                    w = open_job(l, "oT", i)
                    for pair in range(2):
                        for half in range(2):
                            h = 4 * i + 2 * pair + half
                            dst = w[half * V_DIM:(half + 1) * V_DIM, pair * SEQ:(pair + 1) * SEQ]
                            vh = slice(h * V_DIM, (h + 1) * V_DIM)
                            pe.matmul(dst, V[:, 0, vh], pT[:, h, 0:SEQ], start=True, stop=False)
                            mm = pe.matmul(dst[:, P:SEQ], V[:, 1, vh], pT[:, h, SEQ:3 * P], start=False, stop=True)
                    close_job(mm, "oT", i)
                s = wait_load(uses, "conv_out")
                pe.wait_ge(conv_ready, l + 1)
                for i in range(4):
                    by_feature(l, "ya", i, z, chunks(s, 4, D_MODEL), i * 2 * P)
                s = wait_load(uses, "attn_out")
                wait_stages(l, "oT")
                for i in range(4):
                    by_feature(l, "yb", i, oT, chunks(s, 4, D_MODEL), i * 2 * P)
                pe.wait_ge(y_ready, l * 4 + 4)
                for i in range(4):
                    s = wait_load(uses, f"mix{i // 2}")
                    by_token(l, "mix", i, i % 2, yT, chunks(s, KC, BANK), BANK)
                for i in range(4):
                    s = wait_load(uses, f"xk{i // 2}")
                    by_feature(l, "xk", i, memT, chunks(s, KC, BANK), (i % 2) * 2 * P)
                transpose_norm(l, "xT1", 0)
                wait_stages(l, "xT1")
                for i in range(4):
                    s = wait_load(uses, f"xq{i // 2}")
                    by_feature(l, "xq", i, XT, chunks(s, KC, BANK), (i % 2) * 2 * P)
                wait_stages(l, "xk", "xq")
                for h in range(X_HEADS):
                    w = open_job(l, "xscores", h)
                    for t in range(TT):
                        mm = accumulate(w[:, t * MEM_LEN:(t + 1) * MEM_LEN],
                                        [(xqT[:, 2 * h + c, t * P:(t + 1) * P], xkT[:, 2 * h + c, :]) for c in range(2)])
                    close_job(mm, "xscores", h)
                for i in range(4):
                    s = wait_load(uses, f"xv{i // 2}")
                    by_token(l, "xv", i, i % 2, memT, chunks(s, KC, BANK), BANK)
                for h in range(X_HEADS):
                    pe.wait_ge(xprobs_ready, l * X_HEADS + (h + 1))
                    w = open_job(l, "xpT", h)
                    for m in range(2):
                        for t in range(TT):
                            at = t * MEM_LEN + m * P
                            mm = pe.transpose(w[:, (m * TT + t) * P:(m * TT + t + 1) * P], xS[:, h, at:at + P], ident[:, :])
                    close_job(mm, "xpT", h)
                wait_stages(l, "xpT", "xv")
                for h in range(X_HEADS):
                    w = open_job(l, "xoT", h)
                    for c in range(2):
                        cols = slice(h * X_DIM + c * P, h * X_DIM + (c + 1) * P)
                        mm = accumulate(w[:, c * SEQ:(c + 1) * SEQ], [(xV[:, m, cols], xpT[:, h, m, :]) for m in range(2)])
                    close_job(mm, "xoT", h)
                wait_stages(l, "xoT")
                for i in range(4):
                    s = wait_load(uses, f"xo{i // 2}")
                    by_token(l, "xo", i, i % 2, xoT, chunks(s, KC, BANK), BANK)
                transpose_norm(l, "xT2", 1)
                wait_stages(l, "xT2")
                s = wait_load(uses, "down_router")
                w_down_sb, w_router_sb = chunks(s, 2, D_MODEL), chunks(s, KC, EXPERTS, 2 * D_MODEL)
                w = open_job(l, "router")
                for t in range(TT):
                    mm = accumulate(w[:, t * EXPERTS:(t + 1) * EXPERTS],
                                    [(XT[:, c, t * P:(t + 1) * P], w_router_sb[:, c, :]) for c in range(KC)])
                close_job(mm, "router")
                s = wait_load(uses, "shared")
                for i in range(2):
                    by_feature(l, "shared", i, XT, chunks(s, KC, EXPERT_DIM, i * SLOT // 2))
                wait_stages(l, "shared")
                for t in range(TT):
                    for half in range(2):
                        for c in range(2):
                            mm = pe.matmul(moe_sum[2 * t + half][:, :], sharedT[:, c, t * P:(t + 1) * P],
                                      w_down_sb[:, c, half * BANK:(half + 1) * BANK],
                                      start=(c == 0), stop=False, skip_group_check=True)
                mm.then_inc(shared_down, 1)
                pe.wait_ge(chosen_ready, l + 1)
                w = open_job(l, "place")
                accumulate(w[:, 0:EXPERTS], [(earlier[:, :], chosen[:, 0, :])])
                accumulate(w[:, EXPERTS:2 * EXPERTS], [(ones, chosen[:, 0, :]), (earlier[:, :], chosen[:, 1, :])])
                mm = accumulate(w[:, 2 * EXPERTS:3 * EXPERTS], [(ones, chosen[:, 0, :]), (ones, chosen[:, 1, :])])
                close_job(mm, "place")

                def transpose_sel(b, gathers, first=False):
                    pe.wait_ge(sel_ready, gathers + l)
                    if not first:
                        pe.wait_ge(gather_ready[1], gathers - 1)
                    for t in range(TT):
                        pe.transpose(work[3][:, t * P:(t + 1) * P], sel[b][:, t, :], ident[:, :])
                    for t in range(TT):
                        mm = pe.matmul(work[3][:, SEQ:SEQ + 2], sel[b][:, t, :], gpair[b][:, t, :],
                                       start=(t == 0), stop=(t == TT - 1))
                    mm.then_inc(selT_filled, 1)

                def gather(b, half):
                    w = work[0] if half == 0 else work[3]
                    for c in range(4):
                        for t in range(TT):
                            mm = pe.matmul(w[:, c * P:(c + 1) * P], X[:, t, 4 * half + c::KC], sel[b][:, t, :],
                                           start=(t == 0), stop=(t == TT - 1))
                    mm.then_inc(gather_filled[half], 1)

                for b in range(WORK):
                    last = SETUP_USES + max(n for n in range(FIRST_JOB["xT3"]) if n % WORK == b) // WORK + 1
                    if last > seen.get(b, -1):
                        pe.wait_ge(taken[b], l * BANK_USES[b] + last)
                        seen[b] = last
                pe.wait_ge(ln_applied, l * 3 + 3)
                before = pe.snap(base * 2 + l)
                transpose_sel(0, before + 1, first=True)
                gather(0, 0)
                pe.wait_ge(selT_ready, before + 1)
                gather(0, 1)
                pe.reg_mov(more, 1)
                with pe.Fori(0, more) as r:
                    with pe.Fori(0, BODIES) as i:
                        body = pe.snap(base + r * BODIES + i)
                        loaded = pe.snap((body + (l + 1) * DENSE_USES) * 32)
                        pairs = pe.snap(body * 2)
                        gathers = pe.snap(pairs + l)
                        for j in range(2):
                            pe.wait_ge(gather_ready[0], gathers + (j + 1))
                            pe.wait_ge(gather_ready[1], gathers + (j + 1))
                            for e in range(2):
                                pe.wait_ge(slot_loaded[3 * j + e], loaded + 32)
                            for c in range(KC):
                                for e in range(2):
                                    wgu = ring[:, 3 * j + e, :].rearrange("p (w k n) -> p w k n", w=2, k=KC)
                                    mm = pe.matmul(work[0][e * SLOTS:(e + 1) * SLOTS, :],
                                                   xg[j][:, c, e * SLOTS:(e + 1) * SLOTS], wgu[:, :, c, :],
                                                   start=(c == 0), stop=(c == KC - 1))
                            mm.then_inc(gate_up_done, 1)
                            transpose_sel(1 - j, gathers + (j + 2))
                            pe.wait_ge(hid_ready, pairs + (j + 1))
                            for c in range(2):
                                mm = pe.transpose(work[1][:, c * P:(c + 1) * P], hid[:, c * P:(c + 1) * P], ident[:, :])
                            mm.then_inc(hidT_filled, 1)
                            gather(1 - j, 0)
                            pe.wait_ge(hidT_ready, pairs + (j + 1))
                            pe.wait_ge(slot_loaded[3 * j + 2], loaded + 32)
                            for half in range(2):
                                w = work[2 - half]
                                for c in range(2):
                                    for e in range(2):
                                        wd = chunks(3 * j + 2, 2, D_MODEL, e * SLOT // 2)
                                        mm = pe.matmul(w[e * SLOTS:(e + 1) * SLOTS, :],
                                                       hidT[:, c, e * SLOTS:(e + 1) * SLOTS],
                                                       wd[:, c, half * BANK:(half + 1) * BANK],
                                                       start=(c == 0), stop=(c == 1))
                                mm.then_inc(down_filled[half], 1)
                            pe.wait_ge(selT_ready, gathers + (j + 2))
                            gather(1 - j, 1)
                            for half in range(2):
                                pe.wait_ge(hi_ready[half], pairs + (j + 1))
                                pe.wait_ge(lo_ready[half], pairs + (j + 1))
                                cols = slice(half * BANK, (half + 1) * BANK)
                                for t in range(TT):
                                    for part in (out_hi, out_lo):
                                        mm = pe.matmul(moe_sum[2 * t + half][:, :], selT[:, j, t * P:(t + 1) * P],
                                                       part[:, cols], start=False, stop=False, skip_group_check=True)
                            mm.then_inc(scattered, 1)
                    alone(pe, routing_ready, l + 1)
                    pe.reg_load(more, rounds[0:1, bass.ds(l, 1)])
                done = pe.value_load(bodies[0:1, bass.ds(l + 1, 1)], min_val=0, max_val=4 * BODIES * DEPTH)
                for half in range(2):
                    pe.wait_ge(gather_ready[half], done * 2 + (l + 1))
                transpose_norm(l, "xT3", 2)
                wait_stages(l, "xT3")

        @block.scalar
        def _(act):
            step, tell, take, settle, restart = ordered(act, act_order)

            act.wait_ge(angles_ready, 1)
            act.activation(sin[:, :, :], ang[:, 3, :].rearrange("p (t f) -> p t f", t=TT), ACT.Sin)
            act.activation(cos[:, :, :], ang[:, 3, :].rearrange("p (t f) -> p t f", t=TT), ACT.Sin,
                           scale=0.5).then_inc(sines_ready, 1)

            def norm_transposed(l, stage, which):
                for i in (0, 2):
                    w = wait_filled(act, l, stage, i)
                    for c in range(2):
                        k = PAR_LN + 2 * which * KC + 2 * i + c
                        ins = act.activation(XT[:, 2 * i + c, :], w[:, c * SEQ:(c + 1) * SEQ], ACT.Identity,
                                             scale=par[:, k:k + 1], bias=par[:, k + KC:k + KC + 1])
                        if c == 0:
                            step(ins)
                    take(ins, l, stage, i)

            more = act.alloc_register("act_rounds")
            act.wait_ge(consts_ready, 1)
            with act.Fori(0, DEPTH) as l:
                base = act.value_load(bodies[0:1, bass.ds(l, 1)], min_val=0, max_val=4 * BODIES * DEPTH)
                junk = view(9 * K, Q_RANK)
                for i, (stage, n) in enumerate((("cq", Q_RANK), ("cq", Q_RANK), ("ckv", KV_RANK), ("ckv", KV_RANK))):
                    w = wait_filled(act, l, stage, i % 2)
                    settle()
                    tell(act.activation(junk[:, 0:n], w[:, 0:n], ACT.Square, scale=n ** -0.5,
                                        accum_out=sumsq[:, i:i + 1]),
                         squares_ready, l * 4 + i + 1)
                for i in range(2):
                    w = wait_filled(act, l, "c", i)
                    take(act.copy(c_sb[:, 2 * i:2 * i + 2, :], w[:, :].rearrange("p (m t) -> p m t", m=2)), l, "c", i)
                for i in range(2):
                    w = wait_filled(act, l, "b", i)
                    take(act.copy(b_sb[:, 2 * i:2 * i + 2, :], w[:, :].rearrange("p (m t) -> p m t", m=2)), l, "b", i)
                for i in range(4):
                    w = wait_filled(act, l, "uq", i)
                    take(act.copy(q_cat[:, i // 2, 4 * (i % 2):4 * (i % 2) + 4, :],
                                  w[:, 0:Q_RANK].rearrange("p (h d) -> p h d", h=4)), l, "uq", i)
                for t in range(TT):
                    w = wait_filled(act, l, "uk", t)
                    take(act.copy(k_cat[:, t, :, 0:NOPE], w[:, :].rearrange("p (h d) -> p h d", h=HEADS)), l, "uk", t)
                for t in range(TT):
                    w = wait_filled(act, l, "uv", t)
                    take(act.copy(V[:, t, :], w[:, :]), l, "uv", t)
                for i in range(2):
                    w = wait_filled(act, l, "ga0", i)
                    take(act.activation(sgA[:, 2 * i:2 * i + 2, :], w[:, :].rearrange("p (m t) -> p m t", m=2),
                                        ACT.Sigmoid), l, "ga0", i)
                for i in range(0, 8, 2):
                    t, g = i // 2 % 2, i // 4
                    w = wait_filled(act, l, "qkT", i)
                    take(act.copy(qT[0:QK, 4 * g:4 * g + 4, t * P:(t + 1) * P],
                                  w[0:QK, :].rearrange("p (h t) -> p h t", h=4)), l, "qkT", i)

                def exps(g):
                    act.wait_ge(max_ready, l * 2 + (g + 1))
                    for h in range(4 * g, 4 * g + 4):
                        for t, cols in ((0, slice(0, P)), (1, slice(P, 3 * P))):
                            ins = act.activation(S[:, h, cols], S[:, h, cols], ACT.Exp, scale=MLA_SCALE,
                                                 bias=row_max[:, h, t:t + 1], accum_out=row_sum[:, h, t:t + 1])
                    ins.then_inc(exp_ready, 1)

                exps(0)
                exps(1)
                for i in range(2):
                    w = wait_filled(act, l, "ga1", i)
                    take(act.activation(sgA[:, 4 + 2 * i:6 + 2 * i, :], w[:, :].rearrange("p (m t) -> p m t", m=2),
                                        ACT.Sigmoid), l, "ga1", i)
                act.wait_ge(conv_ready, l + 1)
                for i in range(4):
                    w = wait_filled(act, l, "gb", i)
                    take(act.activation(sgB[:, 2 * i:2 * i + 2, :], w[:, :].rearrange("p (m t) -> p m t", m=2),
                                        ACT.Sigmoid), l, "gb", i)
                for h in range(0, HEADS, 2):
                    w = wait_filled(act, l, "pT", h)
                    take(act.copy(pT[:, h, :], w[:, 0:3 * P]), l, "pT", h)
                w = wait_filled(act, l, "oT", 0)
                take(act.copy(oT[:, 0:2, :], w[:, :].rearrange("p (a t) -> p a t", a=2)), l, "oT", 0)
                for i in range(4):
                    w = wait_filled(act, l, "xk", i)
                    take(act.copy(xkT[:, 2 * i:2 * i + 2, :], w[:, :].rearrange("p (m t) -> p m t", m=2)), l, "xk", i)
                norm_transposed(l, "xT1", 0)
                for i in range(4):
                    w = wait_filled(act, l, "xq", i)
                    take(act.copy(xqT[:, 2 * i:2 * i + 2, :], w[:, :].rearrange("p (m t) -> p m t", m=2)), l, "xq", i)
                for h in range(X_HEADS):
                    act.wait_ge(xmax_ready, l * X_HEADS + (h + 1))
                    w = wait_filled(act, l, "xscores", h)
                    for t in range(TT):
                        cols = slice(t * MEM_LEN, (t + 1) * MEM_LEN)
                        ins = act.activation(xS[:, h, cols], w[:, cols], ACT.Exp, scale=X_SCALE,
                                             bias=row_max[:, h, t:t + 1], accum_out=row_sum[:, h, t:t + 1])
                    take(ins, l, "xscores", h)
                for i in range(4):
                    w = wait_filled(act, l, "xv", i)
                    take(act.copy(xV[:, i % 2, (i // 2) * BANK:(i // 2 + 1) * BANK], w[:, :]), l, "xv", i)
                for h in range(0, X_HEADS, 2):
                    w = wait_filled(act, l, "xpT", h)
                    take(act.copy(xpT[:, h, :, :], w[:, :].rearrange("p (m t) -> p m t", m=2)), l, "xpT", h)
                for h in range(0, X_HEADS, 2):
                    w = wait_filled(act, l, "xoT", h)
                    take(act.copy(xoT[:, 2 * h:2 * h + 2, :], w[:, :].rearrange("p (m t) -> p m t", m=2)), l, "xoT", h)
                norm_transposed(l, "xT2", 1)
                w = wait_filled(act, l, "router")
                take(act.activation(score, w[:, 0:TT * EXPERTS].rearrange("p (t e) -> p t e", t=TT), ACT.Sigmoid),
                     l, "router")
                w = wait_filled(act, l, "shared", 0)
                take(act.activation(shared_act, w[:, :].rearrange("p (m t) -> p m t", m=2), ACT.Silu),
                     l, "shared", 0)

                def take_sel(b, gathers):
                    act.wait_ge(selT_filled, gathers)
                    act.copy(selT[:, b, :], work[3][:, 0:SEQ])
                    act.copy(slot_gate[0:SLOTS, b:b + 1], work[3][0:SLOTS, SEQ:SEQ + 1])
                    act.copy(slot_gate[SLOTS:P, b:b + 1], work[3][SLOTS:P, SEQ + 1:SEQ + 2]).then_inc(selT_ready, 1)

                def take_gather(b, gathers):
                    act.wait_ge(gather_filled[0], gathers)
                    act.copy(xg[b][:, 0:4, :], work[0][:, :].rearrange("p (c s) -> p c s", c=4)
                             ).then_inc(gather_ready[0], 1)

                before = act.snap(base * 2 + l)
                take_sel(0, before + 1)
                take_gather(0, before + 1)
                act.reg_mov(more, 1)
                with act.Fori(0, more) as r:
                    with act.Fori(0, BODIES) as i:
                        pairs = act.snap((base + r * BODIES + i) * 2)
                        gathers = act.snap(pairs + l)
                        for j in range(2):
                            act.wait_ge(gate_up_done, pairs + (j + 2))
                            act.activation(act_gate, work[0][:, 0:EXPERT_DIM], ACT.Silu).then_inc(silu_ready, 1)
                            take_sel(1 - j, gathers + (j + 2))
                            take_gather(1 - j, gathers + (j + 2))
                            for half in range(2):
                                act.wait_ge(down_filled[half], pairs + (j + 1 + half))
                                act.copy(out_hi[:, half * BANK:(half + 1) * BANK], work[2 - half][:, :]
                                         ).then_inc(hi_ready[half], 1)
                    alone(act, routing_ready, l + 1)
                    act.reg_load(more, rounds[0:1, bass.ds(l, 1)])
                norm_transposed(l, "xT3", 2)
                restart()

        @block.vector
        def _(dve):
            step, tell, take, settle, restart = ordered(dve, dve_order)

            def then(ins):
                step(ins)
                settle()

            dve.wait_ge(small_loaded, (1 + 3 * DEPTH + 7) * 16)
            dve.wait_ge(consts_ready, 2)
            then(dve.tensor_copy(pos_f, pos_i[:, :]))
            a3 = [ang[:, i, :].rearrange("p (t f) -> p t f", t=TT) for i in range(4)]
            then(dve.tensor_tensor(a3[0], pos_f.unsqueeze(2).to_broadcast([P, TT, HALF_ROPE]),
                                   inv_freq[:, :].unsqueeze(1).to_broadcast([P, TT, HALF_ROPE]), ALU.mult))
            magic = 1.5 * 2.0 ** 23
            then(dve.tensor_scalar(ang[:, 1, :], ang[:, 0, :], 1.0 / (2.0 * np.pi), magic, ALU.mult, ALU.add))
            then(dve.tensor_scalar(ang[:, 1, :], ang[:, 1, :], -magic, None, ALU.add))
            c1 = 6.28125
            c2 = float(np.float32(np.floor((2 * np.pi - c1) * 2.0 ** 19) / 2.0 ** 19))
            c3 = float(np.float32(2 * np.pi - c1 - c2))
            for src, dst, c in ((0, 2, c1), (2, 4, c2), (4, 5, c3)):
                then(dve.scalar_tensor_tensor(out=ang[:, dst, :], in0=ang[:, 1, :], scalar=-c, in1=ang[:, src, :],
                                              op0=ALU.mult, op1=ALU.add))
            dve.tensor_scalar(ang[:, 3, :], ang[:, 5, :], 3.1415925, -3.1415925, ALU.min, ALU.max
                              ).then_inc(angles_ready, 1)
            for n in range(8):
                dve.wait_ge(filled[n % WORK], n // WORK + 1)
                dst = memT if n < 4 else XT
                c = 2 * (n % 4)
                dve.tensor_copy(dst[:, c:c + 2, :], work[n % WORK][:, :].rearrange("p (c t) -> p c t", c=2)
                                ).then_inc(taken[n % WORK], 1)
            dve.wait_ge(sines_ready, 1)
            then(dve.tensor_tensor(cos[:, :, :], cos[:, :, :], cos[:, :, :], ALU.mult))
            then(dve.tensor_scalar(cos[:, :, :], cos[:, :, :], -2.0, 1.0, ALU.mult, ALU.add))
            restart()
            dve.wait_ge(x_loaded, 16)

            def residual(l, stage, which):
                dve.wait_ge(ln_applied, l * 3 + which + 1)
                for i in range(4):
                    t, half = i % 2, i // 2
                    cols = slice(half * BANK, (half + 1) * BANK)
                    if stage:
                        w = wait_filled(dve, l, stage, i)
                    else:
                        w = moe_sum[2 * t + half]
                    ins = dve.scalar_tensor_tensor(out=X[:, t, cols], in0=X[:, t, cols], scalar=ALPHA, in1=w[:, :],
                                                   op0=ALU.mult, op1=ALU.add)
                    if stage:
                        take(ins, l, stage, i)
                    else:
                        step(ins)
                settle()

            def layer_norm(l, which):
                for t in range(TT):
                    for half in range(2):
                        step(dve.bn_stats(stats[:, t, 6 * half:6 * half + 6], X[:, t, half * BANK:(half + 1) * BANK]))
                    settle()
                    tell(dve.bn_aggr(moments[:, 2 * t:2 * t + 2], stats[:, t, :]), moments_ready, l * 6 + (2 * which + t + 1))
                for t in range(TT):
                    dve.wait_ge(ln_rstd_ready, l * 6 + (2 * which + t + 1))
                    tell(dve.tensor_scalar(XN[:, t, :], X[:, t, :], moments[:, 2 * t:2 * t + 1], ln_rstd[:, t:t + 1],
                                           ALU.subtract, ALU.mult), norm_ready, l * 6 + (2 * which + t + 1))

            def norm_transposed(l, stage, which):
                for i in (1, 3):
                    w = wait_filled(dve, l, stage, i)
                    for c in range(2):
                        k = PAR_LN + 2 * which * KC + 2 * i + c
                        ins = dve.tensor_scalar(XT[:, 2 * i + c, :], w[:, c * SEQ:(c + 1) * SEQ],
                                                par[:, k:k + 1], par[:, k + KC:k + KC + 1], ALU.mult, ALU.add)
                        if c == 0:
                            step(ins)
                    take(ins, l, stage, i)

            more = dve.alloc_register("dve_rounds")
            with dve.Fori(0, DEPTH) as l:
                base = dve.value_load(bodies[0:1, bass.ds(l, 1)], min_val=0, max_val=4 * BODIES * DEPTH)
                then(dve.tensor_copy(par[:, :], par_all[:, bass.ds(l, 1), :].rearrange("p o n -> p (o n)")))
                for i in range(4):
                    stage, t = ("cq", "ckv")[i // 2], i % 2
                    n = (Q_RANK, KV_RANK)[i // 2]
                    dve.wait_ge(rstd_ready, l * 4 + (i + 1))
                    w = work[job(stage, t)[0]]
                    if i >= 2:
                        step(dve.tensor_copy(kr[:, t, :], w[:, KV_RANK:KV_RANK + ROPE]))
                    take(dve.tensor_scalar((cqn, ckvn)[i // 2][:, t, :], w[:, 0:n], rstd[:, i:i + 1], None,
                                                ALU.mult), l, stage, t)
                step(dve.memset(u_pad[:, :, 0:2], 0.0))
                for i in range(2):
                    wait_taken(dve, l, "c", 1, i)
                    w = wait_filled(dve, l, "h", i)
                    take(dve.tensor_tensor(u_pad[:, 2 * i:2 * i + 2, 2:], w[:, :].rearrange("p (m t) -> p m t", m=2),
                                                c_sb[:, 2 * i:2 * i + 2, :], ALU.mult), l, "h", i)
                settle()
                for i, chunks_of in enumerate(([(cqT, 0), (cqT, 1)], [(cqT, 2)], [(ckvT, 0), (ckvT, 1)])):
                    w = wait_filled(dve, l, "rankT", i)
                    for j, (dst, c) in enumerate(chunks_of):
                        g = (PAR_Q if dst is cqT else PAR_KV) + c
                        ins = dve.tensor_scalar(dst[:, c, :], w[:, j * SEQ:(j + 1) * SEQ], par[:, g:g + 1], None,
                                                ALU.mult)
                    take(ins, l, "rankT", i)
                for k in range(CONV_WIDTH):
                    for c in range(CONV_DIM // P):
                        g = PAR_CONV + k * (CONV_DIM // P) + c
                        if k == 0:
                            step(dve.tensor_scalar(z[:, c, :], u_pad[:, c, 0:SEQ], par[:, g:g + 1], None, ALU.mult))
                        else:
                            step(dve.scalar_tensor_tensor(out=z[:, c, :], in0=u_pad[:, c, k:k + SEQ], scalar=par[:, g:g + 1],
                                                          in1=z[:, c, :], op0=ALU.mult, op1=ALU.add))
                    settle()
                wait_taken(dve, l, "b")
                tell(dve.tensor_tensor(z, z, b_sb, ALU.mult), conv_ready, l + 1)
                wait_taken(dve, l, "uq")

                def rotate(x1, x2, o1, o2, cs, sn, shape, buf):
                    a, b, c, d = buf
                    step(dve.tensor_tensor(a, x1, cs, ALU.mult))
                    step(dve.tensor_tensor(b, x2, sn, ALU.mult))
                    step(dve.tensor_tensor(c, x2, cs, ALU.mult))
                    step(dve.tensor_tensor(d, x1, sn, ALU.mult))
                    settle()
                    step(dve.tensor_tensor(o1, a, b, ALU.subtract))
                    step(dve.tensor_tensor(o2, c, d, ALU.add))

                for t in range(TT):
                    shape = [P, HEADS, HALF_ROPE]
                    cs = cos[:, t:t + 1, :].to_broadcast(shape)
                    sn = sin[:, t:t + 1, :].to_broadcast(shape)
                    buf = [rope_t[:, i, t * HEADS * HALF_ROPE:(t + 1) * HEADS * HALF_ROPE]
                           .rearrange("p (h f) -> p h f", h=HEADS) for i in range(4)]
                    x1, x2 = q_cat[:, t, :, NOPE:NOPE + HALF_ROPE], q_cat[:, t, :, NOPE + HALF_ROPE:QK]
                    rotate(x1, x2, x1, x2, cs, sn, shape, buf)
                settle()
                shape = [P, TT, HALF_ROPE]
                buf = [rope_t[:, i, 0:TT * HALF_ROPE].rearrange("p (t f) -> p t f", t=TT) for i in range(4)]
                x1, x2 = kr[:, :, 0:HALF_ROPE], kr[:, :, HALF_ROPE:ROPE]
                rotate(x1, x2, x1, x2, cos[:, :, :], sin[:, :, :], shape, buf)
                settle()
                wait_taken(dve, l, "uk")
                for t in range(TT):
                    ins = dve.tensor_copy(k_cat[:, t, :, NOPE:QK], kr[:, t:t + 1, :].to_broadcast([P, HEADS, ROPE]))
                    if t == 0:
                        step(ins)
                    else:
                        tell(ins, qk_ready, l + 1)
                for i in range(1, 8, 2):
                    t, g = i // 2 % 2, i // 4
                    w = wait_filled(dve, l, "qkT", i)
                    take(dve.tensor_copy(kT[0:QK, 4 * g:4 * g + 4, t * P:(t + 1) * P],
                                         w[0:QK, :].rearrange("p (h t) -> p h t", h=4)), l, "qkT", i)
                def maxima(g):
                    for h in range(4 * g, 4 * g + 4):
                        w = wait_filled(dve, l, "scores", h)
                        take(dve.tensor_tensor(S[:, h, :], w[:, 0:3 * P], mask[:, :], ALU.add), l, "scores", h)
                    settle()
                    hs = slice(4 * g, 4 * g + 4)
                    step(dve.tensor_reduce(row_max[:, hs, 0], S[:, hs, 0:P], AX_X, ALU.max))
                    step(dve.tensor_reduce(row_max[:, hs, 1], S[:, hs, P:3 * P], AX_X, ALU.max))
                    settle()
                    tell(dve.tensor_scalar(row_max[:, hs, :], row_max[:, hs, :], -MLA_SCALE, None, ALU.mult),
                         max_ready, l * 2 + (g + 1))

                def normalize(g):
                    hs = slice(4 * g, 4 * g + 4)
                    dve.wait_ge(exp_ready, l * 2 + (g + 1))
                    then(dve.reciprocal(row_sum[:, hs, :], row_sum[:, hs, :]))
                    step(dve.tensor_tensor(S[:, hs, 0:P], S[:, hs, 0:P],
                                           row_sum[:, hs, 0:1].to_broadcast([P, 4, P]), ALU.mult))
                    tell(dve.tensor_tensor(S[:, hs, P:3 * P], S[:, hs, P:3 * P],
                                           row_sum[:, hs, 1:2].to_broadcast([P, 4, 2 * P]), ALU.mult),
                         probs_ready, l * 2 + (g + 1))

                maxima(0)
                maxima(1)
                normalize(0)
                normalize(1)
                for h in range(1, HEADS, 2):
                    w = wait_filled(dve, l, "pT", h)
                    take(dve.tensor_copy(pT[:, h, :], w[:, 0:3 * P]), l, "pT", h)
                w = wait_filled(dve, l, "oT", 1)
                take(dve.tensor_copy(oT[:, 2:4, :], w[:, :].rearrange("p (a t) -> p a t", a=2)), l, "oT", 1)
                wait_taken(dve, l, "ga0")
                wait_taken(dve, l, "ga1")
                for i in range(4):
                    w = wait_filled(dve, l, "ya", i)
                    cs = slice(2 * i, 2 * i + 2)
                    take(dve.tensor_tensor(yT[:, cs, :], w[:, :].rearrange("p (m t) -> p m t", m=2), sgA[:, cs, :],
                                                ALU.mult), l, "ya", i)
                wait_taken(dve, l, "gb")
                for i in range(4):
                    w = wait_filled(dve, l, "yb", i)
                    cs = slice(2 * i, 2 * i + 2)
                    take(dve.tensor_tensor(sgB[:, cs, :], w[:, :].rearrange("p (m t) -> p m t", m=2), sgB[:, cs, :],
                                                ALU.mult), l, "yb", i)
                    settle()
                    tell(dve.tensor_tensor(yT[:, cs, :], yT[:, cs, :], sgB[:, cs, :], ALU.add),
                         y_ready, l * 4 + (i + 1))
                residual(l, "mix", 0)
                layer_norm(l, 0)
                norm_transposed(l, "xT1", 0)
                for h in range(X_HEADS):
                    w = wait_filled(dve, l, "xscores", h)
                    then(dve.tensor_reduce(row_max[:, h, :], w[:, :].rearrange("p (t m) -> p t m", t=TT), AX_X, ALU.max))
                    tell(dve.tensor_scalar(row_max[:, h, :], row_max[:, h, :], -X_SCALE, None, ALU.mult),
                         xmax_ready, l * X_HEADS + (h + 1))
                for h in range(X_HEADS):
                    wait_taken(dve, l, "xscores", 1, h)
                    then(dve.reciprocal(row_sum[:, h, :], row_sum[:, h, :]))
                    xs = xS[:, h, :].rearrange("p (t m) -> p t m", t=TT)
                    tell(dve.tensor_tensor(xs, xs, row_sum[:, h, :].unsqueeze(2).to_broadcast([P, TT, MEM_LEN]),
                                           ALU.mult), xprobs_ready, l * X_HEADS + (h + 1))
                for h in range(1, X_HEADS, 2):
                    w = wait_filled(dve, l, "xpT", h)
                    take(dve.tensor_copy(xpT[:, h, :, :], w[:, :].rearrange("p (m t) -> p m t", m=2)), l, "xpT", h)
                for h in range(1, X_HEADS, 2):
                    w = wait_filled(dve, l, "xoT", h)
                    take(dve.tensor_copy(xoT[:, 2 * h:2 * h + 2, :], w[:, :].rearrange("p (m t) -> p m t", m=2)), l, "xoT", h)
                residual(l, "xo", 1)
                layer_norm(l, 1)
                norm_transposed(l, "xT2", 1)
                step(dve.memset(ones, 1.0))
                step(dve.tensor_scalar(before_group, iota[:, 0:GROUPS].unsqueeze(1).to_broadcast([P, GROUPS, GROUPS]),
                                       1.0, None, ALU.mult))
                settle()
                step(dve.tensor_tensor(before_group, before_group,
                                       iota[:, 0:GROUPS].unsqueeze(2).to_broadcast([P, GROUPS, GROUPS]), ALU.is_lt))
                wait_taken(dve, l, "router")
                bias = par[:, PAR_BIAS:PAR_BIAS + EXPERTS].unsqueeze(1).to_broadcast([P, TT, EXPERTS])
                then(dve.tensor_tensor(biased, score, bias, ALU.add))
                for t in range(TT):
                    for g in range(GROUPS):
                        step(dve.max(top2[:, t * GROUPS + g, :], biased[:, t, g * 8:(g + 1) * 8]))
                settle()
                then(dve.tensor_tensor(group_score, top2[:, :, 0], top2[:, :, 1], ALU.add))
                for t in range(TT):
                    gs = group_score[:, t * GROUPS:(t + 1) * GROUPS]
                    other = gs.unsqueeze(1).to_broadcast([P, GROUPS, GROUPS])
                    own = gs.unsqueeze(2).to_broadcast([P, GROUPS, GROUPS])
                    rows = slice(t * GROUPS, (t + 1) * GROUPS)
                    step(dve.tensor_tensor(cmp_a[:, rows, :], other, own, ALU.is_gt))
                    then(dve.tensor_tensor(cmp_b[:, rows, :], other, own, ALU.is_equal))
                    then(dve.tensor_tensor(cmp_b[:, rows, :], cmp_b[:, rows, :], before_group, ALU.mult))
                    then(dve.tensor_tensor(cmp_a[:, rows, :], cmp_a[:, rows, :], cmp_b[:, rows, :], ALU.add))
                then(dve.tensor_reduce(group_rank, cmp_a, AX_X, ALU.add))
                then(dve.tensor_scalar(penalty[:, :], group_rank, TOP_GROUPS - 0.5, MASKED, ALU.is_gt, ALU.mult))
                then(dve.tensor_tensor(masked.rearrange("p t (g e) -> p (t g) e", g=GROUPS),
                                       biased.rearrange("p t (g e) -> p (t g) e", g=GROUPS),
                                       penalty[:, :].unsqueeze(2).to_broadcast([P, TT * GROUPS, EXPERTS // GROUPS]),
                                       ALU.add))
                for t in range(TT):
                    then(dve.max(top8[:, t, :], masked[:, t, :]))
                    step(dve.match_replace(marked[:, t, :], top8[:, t, :], masked[:, t, :], TAKEN))
                settle()
                tell(dve.tensor_scalar(chosen, marked, TAKEN, None, ALU.is_equal), chosen_ready, l + 1)
                settle()
                then(dve.tensor_tensor(weight, score, chosen, ALU.mult))
                then(dve.tensor_reduce(gate_sum[:, :], weight, AX_X, ALU.add))
                then(dve.reciprocal(gate_sum[:, :], gate_sum[:, :]))
                then(dve.tensor_scalar(gate_sum[:, :], gate_sum[:, :], ROUTE_SCALE, None, ALU.mult))
                then(dve.tensor_tensor(gates[:, :, 0:EXPERTS], weight,
                                       gate_sum[:, :].unsqueeze(2).to_broadcast([P, TT, EXPERTS]), ALU.mult))
                step(dve.tensor_copy(gates[:, :, EXPERTS:PADDED], gates[:, :, 0:4]))
                wait_taken(dve, l, "shared", 1)
                w = wait_filled(dve, l, "shared", 1)
                take(dve.tensor_tensor(sharedT, shared_act, w[:, :].rearrange("p (m t) -> p m t", m=2), ALU.mult),
                     l, "shared", 1)
                w = wait_filled(dve, l, "place")
                then(dve.tensor_scalar(pos[:, :, 0:EXPERTS], chosen, -FAR, FAR, ALU.mult, ALU.add))
                step(dve.tensor_tensor(pos[:, :, 0:EXPERTS], pos[:, :, 0:EXPERTS],
                                       w[:, 0:2 * EXPERTS].rearrange("p (t e) -> p t e", t=TT), ALU.add))
                take(dve.tensor_reduce(busiest[:, 0:1], w[:, 2 * EXPERTS:3 * EXPERTS], AX_X, ALU.max), l, "place")
                settle()
                step(dve.tensor_scalar(pos[:, :, EXPERTS:PADDED], pos[:, :, 0:4], -float(SLOTS), None, ALU.add))
                then(dve.tensor_scalar(busiest[:, 1:2], busiest[:, 0:1], float(SLOTS), 1.0, ALU.is_gt, ALU.add))
                for n in range(2, SEQ // SLOTS):
                    then(dve.tensor_scalar(busiest[:, 2:3], busiest[:, 0:1], float(n * SLOTS), None, ALU.is_gt))
                    then(dve.tensor_tensor(busiest[:, 1:2], busiest[:, 1:2], busiest[:, 2:3], ALU.add))
                step(dve.tensor_copy(rounds[:, bass.ds(l, 1)], busiest[0:1, 1:2]))
                then(dve.tensor_copy(bodies_f[:, 0:1], bodies[:, bass.ds(l, 1)]))
                then(dve.scalar_tensor_tensor(out=bodies_f[:, 1:2], in0=busiest[0:1, 1:2], scalar=float(BODIES),
                                              in1=bodies_f[:, 0:1], op0=ALU.mult, op1=ALU.add))
                tell(dve.tensor_copy(bodies[:, bass.ds(l + 1, 1)], bodies_f[:, 1:2]), routing_ready, l + 1)

                def build_sel(b, first):
                    dve.tensor_tensor(
                        sel[b].rearrange("p t (e s) -> p t e s", e=2),
                        pos[:, :, first].unsqueeze(3).to_broadcast([P, TT, 2, SLOTS]),
                        iota[:, :].unsqueeze(1).unsqueeze(1).to_broadcast([P, TT, 2, SLOTS]), ALU.is_equal)
                    dve.tensor_copy(gpair[b], gates[:, :, first]).then_inc(sel_ready, 1)

                def take_gather(b, gathers):
                    dve.wait_ge(gather_filled[1], gathers)
                    dve.tensor_copy(xg[b][:, 4:8, :], work[3][:, :].rearrange("p (c s) -> p c s", c=4)
                                    ).then_inc(gather_ready[1], 1)

                settle()
                for j in range(2):
                    build_sel(j, slice(2 * j, 2 * j + 2))
                take_gather(0, base * 2 + (l + 1))
                restart()
                dve.reg_mov(more, 1)
                with dve.Fori(0, more) as r:
                    with dve.Fori(0, BODIES) as i:
                        pairs = dve.snap((base + r * BODIES + i) * 2)
                        gathers = dve.snap(pairs + l)
                        for j in range(2):
                            dve.wait_ge(silu_ready, pairs + (j + 1))
                            dve.scalar_tensor_tensor(out=hid, in0=act_gate, scalar=slot_gate[:, j:j + 1],
                                                     in1=work[0][:, EXPERT_DIM:2 * EXPERT_DIM],
                                                     op0=ALU.mult, op1=ALU.mult).then_inc(hid_ready, 1)
                            dve.wait_ge(hidT_filled, pairs + (j + 1))
                            dve.tensor_copy(hidT, work[1][:, 0:2 * P].rearrange("p (c s) -> p c s", c=2)
                                            ).then_inc(hidT_ready, 1)
                            build_sel(j, bass.ds(i * 4 + (2 * j + 4), 2))
                            for half in range(2):
                                cols = slice(half * BANK, (half + 1) * BANK)
                                dve.wait_ge(hi_ready[half], pairs + (j + 1))
                                dve.tensor_tensor(out_lo[:, cols], work[2 - half][:, :], out_hi[:, cols].bitcast(F32),
                                                  ALU.subtract).then_inc(lo_ready[half], 1)
                            take_gather(1 - j, gathers + (j + 2))
                    dve.wait_ge(sel_ready, (base + (r + 1) * BODIES) * 2 + (l * 2 + 2))
                    then(dve.tensor_scalar(pos, pos, -float(SLOTS), None, ALU.add))
                    restart()
                    alone(dve, routing_ready, l + 1)
                    dve.reg_load(more, rounds[0:1, bass.ds(l, 1)])
                done = dve.value_load(bodies[0:1, bass.ds(l + 1, 1)], min_val=0, max_val=4 * BODIES * DEPTH)
                dve.wait_ge(scattered, done * 2)
                residual(l, None, 2)
                layer_norm(l, 2)
                norm_transposed(l, "xT3", 2)
                for i in (2, 3):
                    b, n = job("xT3", i)
                    alone(dve, taken[b], l * BANK_USES[b] + n)
                restart()


_INS = ["x", "mem", "positions", "w_in", "w_conv", "w_conv_out", "q_norm", "w_uq", "kv_norm", "w_uk", "w_uv",
        "w_attn_out", "w_mix_out", "ln1_g", "ln1_b", "w_xq", "w_xk", "w_xv", "w_xo", "ln2_g", "ln2_b",
        "w_router", "router_bias", "w_gate", "w_up", "w_down", "ws_gate", "ws_up", "ws_down", "ln3_g", "ln3_b"]


def kernel(**inputs):
    import numpy as _np
    import concourse.bacc as _bacc
    from concourse import mybir as _mybir
    from concourse.bass_utils import run_bass_kernel_spmd as _run

    nc = _bacc.Bacc("TRN2", target_bir_lowering=False, num_devices=1)
    arrays, args = {}, []
    for name in _INS:
        a = _np.ascontiguousarray(inputs[name])
        arrays[f"in_{name}"] = a
        args.append(nc.dram_tensor(f"in_{name}", a.shape, _mybir.dt.from_np(a.dtype), kind="ExternalInput").ap())
    args.append(nc.dram_tensor("out_0", inputs["x"].shape, _mybir.dt.float32, kind="ExternalOutput").ap())
    build_trunk(nc, *args)
    r = _run(nc, [arrays], core_ids=[0])
    return r.results[0]["out_0"]
```

```python
from contextlib import ExitStack

import numpy as np

import concourse.bass as bass
from concourse import mybir

ALU = mybir.AluOpType
ACT = mybir.ActivationFunctionType
AX_X = mybir.AxisListType.X
F32 = mybir.dt.float32
F32R = mybir.dt.float32r
I32 = mybir.dt.int32

P = 128
D_MODEL = 1024
SEQ = 256
DEPTH = 2
MEM_LEN = 256
CONV_DIM = 512
CONV_WIDTH = 3
HEADS = 8
NOPE = 64
ROPE = 32
HALF_ROPE = ROPE // 2
QK = NOPE + ROPE
V_DIM = 64
Q_RANK = 384
KV_RANK = 256
ROPE_BASE = 10000.0
X_HEADS = 4
X_DIM = D_MODEL // X_HEADS
EXPERTS = 64
TOP_K = 8
GROUPS = 8
TOP_GROUPS = 4
EXPERT_DIM = 256
ROUTE_SCALE = 2.5
LN_EPS = 1e-5
RMS_EPS = 1e-6
ALPHA = (2 * DEPTH) ** 0.25
MLA_SCALE = QK ** -0.5
X_SCALE = X_DIM ** -0.5

TT = SEQ // P
KC = D_MODEL // P
BANK = 512
SLOT = KC * BANK
RING = 6
SLOTS = 64
PAIRS = EXPERTS // 2
BODIES = PAIRS // 2
PADDED = EXPERTS + 4
MASKED = -1e30
FAR = 1e4
TAKEN = 3e30

IN_B, IN_C, IN_H = 0, CONV_DIM, 2 * CONV_DIM
IN_Q = 3 * CONV_DIM
IN_KV = IN_Q + Q_RANK
IN_GA = IN_KV + KV_RANK + ROPE
IN_GB = IN_GA + D_MODEL

STAGES = [
    ("xT0", 4), ("cq", 2), ("ckv", 2), ("c", 2), ("h", 2), ("b", 2), ("rankT", 3), ("uq", 4), ("uk", 2), ("uv", 2),
    ("ga0", 2), ("qkT", 8), ("scores", 8), ("ga1", 2), ("gb", 4), ("pT", 8), ("oT", 2),
    ("ya", 4), ("yb", 4), ("mix", 4), ("xk", 4), ("xT1", 4), ("xq", 4), ("xscores", 4), ("xv", 4),
    ("xpT", 4), ("xoT", 4), ("xo", 4), ("xT2", 4), ("router", 1), ("shared", 2), ("place", 1),
]
WORK = 4
FIRST_JOB, n_jobs = {}, 0
for _name, _count in STAGES:
    FIRST_JOB[_name] = n_jobs
    n_jobs += _count
JOBS = dict(STAGES)
SETUP_USES = 1
BANK_USES = [len(range(b, n_jobs, WORK)) for b in range(WORK)]


def job(stage, i=0):
    assert i < JOBS[stage]
    n = FIRST_JOB[stage] + i
    return n % WORK, SETUP_USES + n // WORK + 1


LOADS = ["cq", "ckv_uv", "c", "h", "b", "uq_uk", "ga0", "ga1", "gb0", "gb1", "conv_out", "attn_out",
         "mix0", "mix1", "xk0", "xk1", "xq0", "xq1", "xv0", "xv1", "xo0", "xo1", "shared", "down_router"]
DENSE_USES = len(LOADS) // RING
assert len(LOADS) % RING == 0

PAR_Q = 0
PAR_KV = PAR_Q + Q_RANK // P
PAR_CONV = PAR_KV + KV_RANK // P
PAR_LN = PAR_CONV + CONV_WIDTH * (CONV_DIM // P)
PAR_BIAS = PAR_LN + 6 * KC
N_PAR = PAR_BIAS + EXPERTS
SMALL_LOADS = 1 + 3 * DEPTH
NORM_LOADS = 7


def build_trunk(nc, x, mem, positions, w_in, w_conv, w_conv_out, q_norm, w_uq, kv_norm, w_uk, w_uv,
                w_attn_out, w_mix_out, ln1_g, ln1_b, w_xq, w_xk, w_xv, w_xo, ln2_g, ln2_b,
                w_router, router_bias, w_gate, w_up, w_down, ws_gate, ws_up, ws_down, ln3_g, ln3_b, out):
    with ExitStack() as ctx:
        def sb(name, shape, dt=F32):
            return ctx.enter_context(nc.sbuf_tensor(name, shape, dt))

        def sem(name):
            return ctx.enter_context(nc.semaphore(name))

        ring = sb("ring", [P, RING, SLOT])
        X = sb("X", [P, TT, D_MODEL])
        XT = sb("XT", [P, KC, SEQ])
        memT = sb("memT", [P, KC, MEM_LEN])
        arena = sb("arena", [P, 18 * 1024])
        out_hi = sb("out_hi", [P, D_MODEL], F32R)
        out_lo = sb("out_lo", [P, D_MODEL], F32R)
        selT = sb("selT", [P, 2, SEQ], F32R)
        ident = sb("ident", [P, P])
        earlier = sb("earlier", [P, P])
        mask = sb("mask", [P, 3 * P])
        iota = sb("iota", [P, SLOTS])
        par_all = sb("par_all", [P, DEPTH, N_PAR])
        par = sb("par", [P, N_PAR])
        cos = sb("cos", [P, TT, HALF_ROPE])
        sin = sb("sin", [P, TT, HALF_ROPE])
        small = sb("small", [P, 96])
        rounds = sb("rounds", [1, DEPTH], I32)
        bodies = sb("bodies", [1, DEPTH + 1], I32)

        def view(at, *shape):
            n = int(np.prod(shape))
            v = arena[:, at:at + n]
            if len(shape) == 2:
                return v.rearrange("p (a b) -> p a b", a=shape[0])
            if len(shape) == 3:
                return v.rearrange("p (a b c) -> p a b c", a=shape[0], b=shape[1])
            return v

        K = 1024
        gb = view(0, 2, D_MODEL)
        XN = view(16 * K, TT, D_MODEL)
        pT = view(0, HEADS, 3 * P)
        cqn = view(0, TT, Q_RANK)
        ckvn = view(768, TT, KV_RANK)
        cqT = view(1280, Q_RANK // P, SEQ)
        ckvT = view(2048, KV_RANK // P, SEQ)
        kr = view(2560, TT, ROPE)
        c_sb = view(2 * K + 640, CONV_DIM // P, SEQ)
        u_pad = view(3 * K + 640, CONV_DIM // P, SEQ + 2)
        b_sb = view(4 * K + 704, CONV_DIM // P, SEQ)
        sgB = view(3 * K, KC, SEQ)
        q_cat = view(6 * K, TT, HEADS, QK)
        k_cat = view(6 * K + 1536, TT, HEADS, QK)
        S = view(6 * K, HEADS, 3 * P)
        yT = view(6 * K, KC, SEQ)
        qT = view(9 * K, HEADS, SEQ)
        kT = view(11 * K, HEADS, SEQ)
        V = view(13 * K, TT, HEADS * V_DIM)
        z = view(14 * K, CONV_DIM // P, SEQ)
        oT = view(15 * K, HEADS // 2, SEQ)
        sgA = view(16 * K, KC, SEQ)
        rope_t = view(11 * K, 4, TT * HEADS * HALF_ROPE)
        xkT = view(2 * K, KC, MEM_LEN)
        xV = view(4 * K, TT, D_MODEL)
        xqT = view(6 * K, KC, SEQ)
        xS = view(8 * K, X_HEADS, TT * MEM_LEN)
        xpT = view(10 * K, X_HEADS, 2, SEQ)
        xoT = view(12 * K, KC, SEQ)
        centred = view(2 * K, TT, D_MODEL)
        xg = [view(2 * K + b * K, KC, P) for b in range(2)]
        sel = [view(4 * K + b * 256, TT, P) for b in range(2)]
        act_gate = view(5 * K - 512, EXPERT_DIM)
        hid = view(5 * K - 256, EXPERT_DIM)
        hidT = view(5 * K, 2, P)
        sharedT = view(5 * K + 256, 2, SEQ)
        shared_act = view(6 * K, 2, SEQ)
        score = view(6 * K + 512, TT, EXPERTS)
        biased = view(6 * K + 640, TT, EXPERTS)
        masked = view(6 * K + 768, TT, EXPERTS)
        marked = view(6 * K + 896, TT, EXPERTS)
        chosen = view(7 * K, TT, EXPERTS)
        weight = view(7 * K + 128, TT, EXPERTS)
        gates = view(7 * K + 256, TT, PADDED)
        pos = view(7 * K + 256 + 2 * PADDED, TT, PADDED)
        top2 = view(7 * K + 768, TT * GROUPS, 8)
        cmp_a = view(8 * K, TT * GROUPS, GROUPS)
        cmp_b = view(8 * K + 128, TT * GROUPS, GROUPS)
        before_group = view(8 * K + 256, GROUPS, GROUPS)
        ones = view(8 * K + 640, P)
        gpair = [view(8 * K + 768 + 4 * b, TT, 2) for b in range(2)]
        ahead = view(9 * K, 2, SLOT)
        mem_sb = view(0, TT, D_MODEL)
        ang = view(2 * K, 8, TT * HALF_ROPE)
        pos_i = sb("pos_i", [P, TT], I32)
        pos_f = small[:, 0:2]
        sumsq = small[:, 2:6]
        rstd = small[:, 6:10]
        row_max = small[:, 10:26].rearrange("p (h t) -> p h t", t=TT)
        row_sum = small[:, 26:42].rearrange("p (h t) -> p h t", t=TT)
        moments = small[:, 54:58]
        ln_rstd = small[:, 90:92]
        ln_shift = small[:, 92:94]
        group_score = small[:, 58:74]
        group_rank = small[:, 74:90]
        top8 = sb("top8", [P, TT, 8])
        gate_sum = sb("gate_sum", [P, TT])
        slot_gate = sb("slot_gate", [P, 2])
        busiest = sb("busiest", [P, 4])
        bodies_f = sb("bodies_f", [1, 2])
        penalty = sb("penalty", [P, TT * GROUPS])
        stats = sb("stats", [P, TT, 12])
        minus_half = sb("minus_half", [P, 1])
        inv_freq = sb("inv_freq", [P, HALF_ROPE])

        work = [ctx.enter_context(nc.psum_tensor(f"work{b}", [P, BANK], F32)) for b in range(WORK)]
        moe_sum = [ctx.enter_context(nc.psum_tensor(f"moe_sum{b}", [P, BANK], F32)) for b in range(4)]

        passed = sem("passed")
        x_loaded = sem("x_loaded")
        mem_loaded = sem("mem_loaded")
        small_loaded = sem("small_loaded")
        norm_loaded = sem("norm_loaded")
        ident_ready = sem("ident_ready")
        consts_ready = sem("consts_ready")
        angles_ready = sem("angles_ready")
        sines_ready = sem("sines_ready")
        slot_loaded = [sem(f"slot_loaded{s}") for s in range(RING)]
        ahead_loaded = sem("ahead_loaded")
        filled = [sem(f"filled{b}") for b in range(WORK)]
        taken = [sem(f"taken{b}") for b in range(WORK)]
        act_order = sem("act_order")
        dve_order = sem("dve_order")
        pool_order = sem("pool_order")
        squares_ready = sem("squares_ready")
        qk_ready = sem("qk_ready")
        conv_ready = sem("conv_ready")
        max_ready = sem("max_ready")
        exp_ready = sem("exp_ready")
        probs_ready = sem("probs_ready")
        y_ready = sem("y_ready")
        rstd_ready = sem("rstd_ready")
        moments_ready = sem("moments_ready")
        ln_rstd_ready = sem("ln_rstd_ready")
        ln_shift_ready = sem("ln_shift_ready")
        norm_ready = [sem("norm_ready_0"), sem("norm_ready_1")]
        ln_loaded = sem("ln_loaded")
        ln_applied = sem("ln_applied")
        layer_done = sem("layer_done")
        xmax_ready = sem("xmax_ready")
        xprobs_ready = sem("xprobs_ready")
        chosen_ready = sem("chosen_ready")
        routing_ready = sem("routing_ready")
        shared_down = sem("shared_down")
        sel_ready = sem("sel_ready")
        gate_up_done = sem("gate_up_done")
        silu_ready = sem("silu_ready")
        hid_ready = sem("hid_ready")
        selT_filled = sem("selT_filled")
        selT_ready = sem("selT_ready")
        hidT_filled = sem("hidT_filled")
        hidT_ready = sem("hidT_ready")
        gather_filled = [sem("gather_filled_a"), sem("gather_filled_b")]
        gather_ready = [sem("gather_ready_a"), sem("gather_ready_b")]
        down_filled = [sem("down_filled_0"), sem("down_filled_1")]
        hi_ready = [sem("hi_ready_0"), sem("hi_ready_1")]
        lo_ready = [sem("lo_ready_0"), sem("lo_ready_1")]
        scattered = sem("scattered")
        out_stored = sem("out_stored")

        def alone(eng, s, value):
            eng.wait_ge(s, value)
            eng.sem_inc(passed, 1)

        def ordered(eng, s):
            n, last = [0], [None]

            def step(ins):
                n[0] += 1
                last[0] = (s, n[0])
                return ins.then_inc(s, 1)

            def tell(ins, semaphore, value):
                last[0] = (semaphore, value)
                return ins.then_inc(semaphore, 1)

            def take(ins, l, stage, i=0):
                b, k = job(stage, i)
                return tell(ins, taken[b], l * BANK_USES[b] + k)

            def settle():
                if last[0]:
                    eng.wait_ge(*last[0])

            def restart():
                if n[0]:
                    eng.wait_ge(s, n[0])
                    eng.sem_clear(s)
                n[0], last[0] = 0, None

            return step, tell, take, settle, restart

        def wait_filled(eng, l, stage, i=0):
            b, n = job(stage, i)
            eng.wait_ge(filled[b], l * BANK_USES[b] + n)
            return work[b]

        def wait_taken(eng, l, stage, count=None, first=0):
            last = {}
            for i in range(first, JOBS[stage] if count is None else first + count):
                b, n = job(stage, i)
                last[b] = n
            for b, n in last.items():
                eng.wait_ge(taken[b], l * BANK_USES[b] + n)

        def chunks(slot, k, n, at=0):
            return ring[:, slot, at:at + k * n].rearrange("p (k n) -> p k n", k=k)

        block = ctx.enter_context(nc.Block())

        @block.sync
        def _(sp):
            x2, m2 = x.rearrange("o s d -> (o s) d"), mem.rearrange("o s d -> (o s) d")
            sp.dma_start(mem_sb, m2.rearrange("(t p) d -> p t d", p=P)).then_inc(mem_loaded, 16)
            sp.dma_start(X[:, :, :], x2.rearrange("(t p) d -> p t d", p=P)).then_inc(x_loaded, 16)
            sp.wait_ge(small_loaded, SMALL_LOADS * 16)
            sp.wait_ge(consts_ready, 1)

            by_feature = {"cq": (IN_Q, Q_RANK), "c": (IN_C, BANK), "h": (IN_H, BANK), "b": (IN_B, BANK),
                          "ga0": (IN_GA, BANK), "ga1": (IN_GA + BANK, BANK),
                          "gb0": (IN_GB, BANK), "gb1": (IN_GB + BANK, BANK)}
            square = {"xk": w_xk, "xq": w_xq, "xv": w_xv}

            def layer_of(w, l):
                return w[bass.ds(l, 1)].rearrange("o k n -> (o k) n")

            def sources(name, l, s):
                if name in by_feature or name[:-1] in square:
                    if name in by_feature:
                        at, n = by_feature[name]
                        w = layer_of(w_in, l)
                    else:
                        at, n = BANK * int(name[-1]), BANK
                        w = layer_of(square[name[:-1]], l)
                    v = w[:, at:at + n].rearrange("(p k) n -> p k n", k=KC)
                    dst = chunks(s, KC, n)
                    return [(dst[:, 0:4], v[:, 0:4]), (dst[:, 4:8], v[:, 4:8])]
                if name == "ckv_uv":
                    n = KV_RANK + ROPE
                    return [(chunks(s, KC, n), layer_of(w_in, l)[:, IN_KV:IN_KV + n].rearrange("(p k) n -> p k n", k=KC)),
                            (chunks(s, 2, 512, KC * n), layer_of(w_uv, l).rearrange("(k p) n -> p k n", p=P))]
                if name == "uq_uk":
                    n = HEADS * QK
                    return [(chunks(s, 3, n), layer_of(w_uq, l).rearrange("(k p) n -> p k n", p=P)),
                            (chunks(s, 2, 512, 3 * n), layer_of(w_uk, l).rearrange("(k p) n -> p k n", p=P))]
                if name in ("conv_out", "attn_out"):
                    w = layer_of(w_conv_out if name == "conv_out" else w_attn_out, l)
                    v = w.rearrange("(k p) n -> p k n", p=P)
                    dst = chunks(s, 4, D_MODEL)
                    return [(dst[:, 0:2], v[:, 0:2]), (dst[:, 2:4], v[:, 2:4])]
                if name in ("mix0", "mix1", "xo0", "xo1"):
                    at = BANK * int(name[-1])
                    w = layer_of(w_mix_out if name[:3] == "mix" else w_xo, l)
                    v = w[:, at:at + BANK].rearrange("(k p) n -> p k n", p=P)
                    dst = chunks(s, KC, BANK)
                    return [(dst[:, 0:4], v[:, 0:4]), (dst[:, 4:8], v[:, 4:8])]
                if name == "shared":
                    return [(chunks(s, KC, EXPERT_DIM), layer_of(ws_gate, l).rearrange("(p k) n -> p k n", k=KC)),
                            (chunks(s, KC, EXPERT_DIM, SLOT // 2), layer_of(ws_up, l).rearrange("(p k) n -> p k n", k=KC))]
                assert name == "down_router"
                return [(chunks(s, 2, D_MODEL), layer_of(ws_down, l).rearrange("(k p) n -> p k n", p=P)),
                        (chunks(s, KC, EXPERTS, 2 * D_MODEL), layer_of(w_router, l).rearrange("(p k) n -> p k n", k=KC))]

            last_job = {"cq": ("cq", 1), "ckv_uv": ("uv", 1), "c": ("c", 1), "h": ("h", 1), "b": ("b", 1),
                        "uq_uk": ("uk", 1), "ga0": ("ga0", 1), "ga1": ("ga1", 1), "gb0": ("gb", 1), "gb1": ("gb", 3),
                        "conv_out": ("ya", 3), "attn_out": ("yb", 3), "shared": ("shared", 1)}
            for stage in ("mix", "xk", "xq", "xv", "xo"):
                last_job[stage + "0"], last_job[stage + "1"] = (stage, 1), (stage, 3)

            def wait_read(l, n):
                if LOADS[n] == "down_router":
                    alone(sp, shared_down, l + 1)
                else:
                    b, k = job(*last_job[LOADS[n]])
                    alone(sp, filled[b], l * BANK_USES[b] + k)

            def load_ln(l, g, b, which):
                sp.wait_ge(ln_applied, l * 3 + which + 1)
                for j, w in ((0, g), (1, b)):
                    sp.dma_start(gb[:, j, :], w[bass.ds(l, 1)].rearrange("o d -> (o d)").partition_broadcast(P)
                                 ).then_inc(ln_loaded, 16)

            e_gate = w_gate.rearrange("l e (p k) f -> (l e) p k f", k=KC)
            e_up = w_up.rearrange("l e (p k) f -> (l e) p k f", k=KC)
            e_down = w_down.rearrange("l e (k p) d -> (l e) p k d", p=P)
            more, start = sp.alloc_register("sp_rounds"), sp.alloc_register("sp_start")
            with sp.Fori(0, DEPTH) as l:
                base = sp.value_load(bodies[0:1, bass.ds(l, 1)], min_val=0, max_val=4 * BODIES * DEPTH)
                for n, name in enumerate(LOADS):
                    s = n % RING
                    if n < RING:
                        alone(sp, down_filled[1] if s % 3 == 2 else gate_up_done, base * 2 + 1)
                    else:
                        wait_read(l, n - RING)
                    if name == "xq1":
                        load_ln(l, ln1_g, ln1_b, 0)
                    for dst, src in sources(name, l, s):
                        sp.dma_start(dst, src).then_inc(slot_loaded[s], 16)
                load_ln(l, ln2_g, ln2_b, 1)

                def load_gate_up(dst, expert, loaded):
                    at = bass.ds(expert, 1)
                    for h, w in enumerate((e_gate, e_up)):
                        sp.dma_start(dst[:, h * SLOT // 2:(h + 1) * SLOT // 2].rearrange("p (k n) -> p k n", k=KC),
                                     w[at].rearrange("o p k f -> (o p) k f")).then_inc(loaded, 16)

                def load_down(s, pair_first):
                    for e in range(2):
                        sp.dma_start(chunks(s, 2, D_MODEL, e * SLOT // 2),
                                     e_down[bass.ds(pair_first + e, 1)].rearrange("o p k d -> (o p) k d")
                                     ).then_inc(slot_loaded[s], 16)

                first = sp.snap(l * EXPERTS)
                for e in range(2):
                    wait_read(l, len(LOADS) - RING + e)
                    sp.sem_inc(slot_loaded[e], 32)
                    load_gate_up(ring[:, e, :], first + (4 + e), slot_loaded[e])
                wait_read(l, len(LOADS) - RING + 2)
                load_down(2, first)
                wait_read(l, len(LOADS) - RING + 3)
                load_gate_up(ring[:, 3, :], first + 2, slot_loaded[3])
                b, n = job("xT2", JOBS["xT2"] - 1)
                alone(sp, filled[b], l * BANK_USES[b] + n)
                alone(sp, ln_applied, l * 3 + 3)
                for e in range(2):
                    load_gate_up(ahead[:, e, :], first + e, ahead_loaded)
                wait_read(l, len(LOADS) - RING + 4)
                load_gate_up(ring[:, 4, :], first + 3, slot_loaded[4])
                wait_read(l, len(LOADS) - RING + 5)
                load_down(5, first + 2)

                def load_pair(l, i, j, pairs, gate_up=True):
                    pair_first = sp.snap(l * EXPERTS + i * 4 + 2 * j)
                    for e in range(2):
                        if gate_up:
                            sp.wait_ge(gate_up_done, pairs + j)
                            load_gate_up(ring[:, 3 * j + e, :], pair_first + e, slot_loaded[3 * j + e])
                    sp.wait_ge(down_filled[1], pairs + j)
                    load_down(3 * j + 2, pair_first)

                pairs = sp.snap((base + 1) * 2)
                load_pair(l, 1, 0, pairs, gate_up=False)
                load_pair(l, 1, 1, pairs)
                sp.reg_mov(more, 1)
                sp.reg_mov(start, 2)
                with sp.Fori(0, more) as r:
                    with sp.Fori(start, BODIES) as i:
                        pairs = sp.snap((base + r * BODIES + i) * 2)
                        for j in range(2):
                            load_pair(l, i, j, pairs)
                    sp.reg_mov(start, 0)
                    alone(sp, routing_ready, l + 1)
                    sp.reg_load(more, rounds[0:1, bass.ds(l, 1)])
                load_ln(l, ln3_g, ln3_b, 2)
            out_tiles = out.rearrange("o (t p) d -> p (o t) d", p=P)
            sp.wait_ge(layer_done, DEPTH)
            sp.dma_start(out_tiles[:, 0, :], X[:, 0, :]).then_inc(out_stored, 16)
            sp.wait_ge(ln_applied, 3 * DEPTH + 1)
            sp.dma_start(out_tiles[:, 1, :], X[:, 1, :]).then_inc(out_stored, 16)
            sp.wait_ge(out_stored, 32)

        @block.gpsimd
        def _(pool):
            step, tell, take, settle, restart = ordered(pool, pool_order)
            tell(pool.memset(bodies[:, :], 0), consts_ready, 1)
            step(pool.memset(ident[:, :], 0.0))
            step(pool.memset(earlier[:, :], 0.0))
            step(pool.memset(mask[:, :], 0.0))
            step(pool.memset(minus_half[:, :], -0.5))
            step(pool.iota(iota[:, :], pattern=[[1, SLOTS]], base=0, channel_multiplier=0,
                           allow_small_or_imprecise_dtypes=True))
            for i in range(HALF_ROPE):
                f = float(np.float32(ROPE_BASE) ** np.float32(-i / HALF_ROPE))
                step(pool.memset(inv_freq[:, i:i + 1], f))
            settle()
            tell(pool.affine_select(out=ident[:, :], in_=ident[:, :], compare_op=ALU.not_equal, fill=1.0,
                                    base=0, pattern=[[-1, P]], channel_multiplier=1), ident_ready, 1)
            step(pool.affine_select(out=earlier[:, :], in_=earlier[:, :], compare_op=ALU.is_ge, fill=1.0,
                                    base=0, pattern=[[-1, P]], channel_multiplier=1))
            for c in (0, 2):
                m = mask[:, c * P:(c + 1) * P]
                ins = pool.affine_select(out=m, in_=m, compare_op=ALU.is_ge, fill=MASKED,
                                         base=0, pattern=[[-1, P]], channel_multiplier=1)
                if c == 0:
                    step(ins)
                else:
                    tell(ins, consts_ready, 2)
            for j, w in enumerate((ln1_g, ln1_b, ln2_g, ln2_b, ln3_g, ln3_b)):
                pool.dma_start(par_all[:, :, PAR_LN + j * KC:PAR_LN + (j + 1) * KC],
                               w.rearrange("l (p k) -> p l k", k=KC)).then_inc(norm_loaded, 16)
            pool.dma_start(par_all[:, :, PAR_BIAS:], router_bias.partition_broadcast(P)).then_inc(norm_loaded, 16)
            restart()
            pool.sem_inc(ln_applied, 1)

            def inverse_root(dst, src, eps, ready):
                step(pool.tensor_scalar(dst, src, eps, None, ALU.add))
                settle()
                pool.tensor_tensor(dst, dst, minus_half[:, :], ALU.pow).then_inc(ready, 1)

            with pool.Fori(0, DEPTH) as l:
                for i in range(4):
                    alone(pool, squares_ready, l * 4 + (i + 1))
                    inverse_root(rstd[:, i:i + 1], sumsq[:, i:i + 1], RMS_EPS, rstd_ready)
                for which in range(3):
                    for t in range(TT):
                        alone(pool, moments_ready, l * 6 + (2 * which + t + 1))
                        inverse_root(ln_rstd[:, t:t + 1], moments[:, 2 * t + 1:2 * t + 2], LN_EPS, ln_rstd_ready)
                        alone(pool, ln_rstd_ready, l * 6 + (2 * which + t + 1))
                        step(pool.tensor_tensor(ln_shift[:, t:t + 1], moments[:, 2 * t:2 * t + 1],
                                                ln_rstd[:, t:t + 1], ALU.mult))
                        settle()
                        pool.tensor_scalar(ln_shift[:, t:t + 1], ln_shift[:, t:t + 1], -1.0, None, ALU.mult
                                           ).then_inc(ln_shift_ready, 1)
                    if which == 2:
                        break
                    for half in range(2):
                        pool.wait_ge(norm_ready[half], l * 6 + 2 * which + 4)
                    pool.wait_ge(ln_loaded, (l * 3 + which + 1) * 32)
                    for t in range(TT):
                        step(pool.tensor_tensor(X[:, t, :], XN[:, t, :], gb[:, 0, :], ALU.mult))
                    settle()
                    for t in range(TT):
                        ins = pool.tensor_tensor(X[:, t, :], X[:, t, :], gb[:, 1, :], ALU.add)
                        if t == 0:
                            step(ins)
                        else:
                            ins.then_inc(ln_applied, 1)
                restart()

        @block.tensor
        def _(pe):
            seen = {}

            def wait_stages(l, *stages):
                last = {}
                for stage in stages:
                    for i in range(JOBS[stage]):
                        b, n = job(stage, i)
                        last[b] = max(n, last.get(b, 0))
                for b, n in last.items():
                    if n > seen.get(b, -1):
                        pe.wait_ge(taken[b], l * BANK_USES[b] + n)
                        seen[b] = n

            def open_job(l, stage, i=0):
                b, n = job(stage, i)
                if n - 1 > seen.get(b, -1):
                    pe.wait_ge(taken[b], l * BANK_USES[b] + (n - 1))
                    seen[b] = n - 1
                return work[b]

            def close_job(mm, stage, i=0):
                mm.then_inc(filled[job(stage, i)[0]], 1)

            def wait_load(uses, name):
                n = LOADS.index(name)
                pe.wait_ge(slot_loaded[n % RING], (uses + (n // RING + 1)) * 32)
                return n % RING

            def accumulate(dst, pairs, l=None, arriving=None):
                for k, (a, b) in enumerate(pairs):
                    if arriving and k % 2 == 0:
                        bank, n = job(arriving, k // 2)
                        if n > seen.get(bank, -1):
                            pe.wait_ge(taken[bank], l * BANK_USES[bank] + n)
                            seen[bank] = n
                    mm = pe.matmul(dst, a, b, start=(k == 0), stop=(k == len(pairs) - 1))
                return mm

            pe.sem_inc(gate_up_done, 1)
            pe.sem_inc(down_filled[1], 1)
            pe.wait_ge(ident_ready, 1)
            pe.wait_ge(mem_loaded, 16)
            for b in range(WORK):
                for c in range(2):
                    for t in range(TT):
                        mm = pe.transpose(work[b][:, (c * TT + t) * P:(c * TT + t + 1) * P],
                                          mem_sb[:, t, 2 * b + c::KC], ident[:, :])
                mm.then_inc(filled[b], 1)
            for b in range(WORK):
                pe.wait_ge(taken[b], SETUP_USES)

            def transpose_norm(l, stage, norms):
                for half in range(2):
                    pe.wait_ge(norm_ready[half], l * 6 + 2 * norms + 2)
                for i in range(4):
                    w = open_job(l, stage, i)
                    for c in range(2):
                        for t in range(TT):
                            mm = pe.transpose(w[:, (c * TT + t) * P:(c * TT + t + 1) * P],
                                              XN[:, t, 2 * i + c::KC], ident[:, :])
                    close_job(mm, stage, i)

            def by_token(l, stage, i, t, src, weights, n, at=0, arriving=None):
                w = open_job(l, stage, i)
                k = weights.shape[1]
                mm = accumulate(w[:, 0:n], [(src[:, c, t * P:(t + 1) * P], weights[:, c, at:at + n]) for c in range(k)],
                                l, arriving)
                close_job(mm, stage, i)

            def by_feature(l, stage, i, src, weights, at=0, arriving=None):
                w = open_job(l, stage, i)
                k = weights.shape[1]
                for m in range(2):
                    cols = slice(at + m * P, at + (m + 1) * P)
                    mm = accumulate(w[:, m * SEQ:(m + 1) * SEQ], [(weights[:, c, cols], src[:, c, :]) for c in range(k)],
                                    l, arriving)
                close_job(mm, stage, i)
                return mm

            more, start = pe.alloc_register("pe_rounds"), pe.alloc_register("pe_start")
            with pe.Fori(0, DEPTH) as l:
                base = pe.value_load(bodies[0:1, bass.ds(l, 1)], min_val=0, max_val=4 * BODIES * DEPTH)
                uses = pe.snap(base + l * DENSE_USES)
                transpose_norm(l, "xT0", 0)
                s = wait_load(uses, "cq")
                for t in range(TT):
                    by_token(l, "cq", t, t, XT, chunks(s, KC, Q_RANK), Q_RANK, arriving="xT0")
                s = wait_load(uses, "ckv_uv")
                for t in range(TT):
                    by_token(l, "ckv", t, t, XT, chunks(s, KC, KV_RANK + ROPE), KV_RANK + ROPE)
                for name in ("c", "h", "b"):
                    s = wait_load(uses, name)
                    for i in range(2):
                        by_feature(l, name, i, XT, chunks(s, KC, BANK), i * 2 * P)
                wait_stages(l, "cq", "ckv")
                for i, blocks in enumerate(([(cqn, 0), (cqn, 1)], [(cqn, 2)], [(ckvn, 0), (ckvn, 1)])):
                    w = open_job(l, "rankT", i)
                    for j, (src, c) in enumerate(blocks):
                        for t in range(TT):
                            mm = pe.transpose(w[:, (j * TT + t) * P:(j * TT + t + 1) * P],
                                              src[:, t, c * P:(c + 1) * P], ident[:, :])
                    close_job(mm, "rankT", i)
                s = wait_load(uses, "uq_uk")
                wait_stages(l, "rankT")
                w_uq_sb = chunks(s, 3, HEADS * QK)
                for i in range(4):
                    by_token(l, "uq", i, i // 2, cqT, w_uq_sb, Q_RANK, (i % 2) * Q_RANK)
                for t in range(TT):
                    by_token(l, "uk", t, t, ckvT, chunks(s, 2, 512, 3 * HEADS * QK), 512)
                s = LOADS.index("ckv_uv") % RING
                for t in range(TT):
                    by_token(l, "uv", t, t, ckvT, chunks(s, 2, 512, KC * (KV_RANK + ROPE)), 512)
                s = wait_load(uses, "ga0")
                for i in range(2):
                    by_feature(l, "ga0", i, XT, chunks(s, KC, BANK), i * 2 * P)
                pe.wait_ge(qk_ready, l + 1)
                for i in range(8):
                    src = (q_cat, k_cat)[i % 2]
                    t, g = i // 2 % 2, i // 4
                    w = open_job(l, "qkT", i)
                    for j in range(4):
                        mm = pe.transpose(w[0:QK, j * P:(j + 1) * P], src[:, t, 4 * g + j, :], ident[:, :])
                    close_job(mm, "qkT", i)
                wait_stages(l, "qkT")
                for h in range(HEADS):
                    w = open_job(l, "scores", h)
                    pe.matmul(w[:, 0:P], qT[0:QK, h, 0:P], kT[0:QK, h, 0:P], start=True, stop=True)
                    mm = pe.matmul(w[:, P:3 * P], qT[0:QK, h, P:SEQ], kT[0:QK, h, :], start=True, stop=True)
                    close_job(mm, "scores", h)
                s = wait_load(uses, "ga1")
                for i in range(2):
                    by_feature(l, "ga1", i, XT, chunks(s, KC, BANK), i * 2 * P)
                for i in range(4):
                    name = f"gb{i // 2}"
                    s = wait_load(uses, name)
                    by_feature(l, "gb", i, XT, chunks(s, KC, BANK), (i % 2) * 2 * P)
                for h in range(HEADS):
                    if h % 4 == 0:
                        pe.wait_ge(probs_ready, l * 2 + (h // 4 + 1))
                    w = open_job(l, "pT", h)
                    for j in range(3):
                        mm = pe.transpose(w[:, j * P:(j + 1) * P], S[:, h, j * P:(j + 1) * P], ident[:, :])
                    close_job(mm, "pT", h)
                wait_stages(l, "pT", "uv")
                for i in range(2):
                    w = open_job(l, "oT", i)
                    for pair in range(2):
                        for half in range(2):
                            h = 4 * i + 2 * pair + half
                            dst = w[half * V_DIM:(half + 1) * V_DIM, pair * SEQ:(pair + 1) * SEQ]
                            vh = slice(h * V_DIM, (h + 1) * V_DIM)
                            pe.matmul(dst, V[:, 0, vh], pT[:, h, 0:SEQ], start=True, stop=False)
                            mm = pe.matmul(dst[:, P:SEQ], V[:, 1, vh], pT[:, h, SEQ:3 * P], start=False, stop=True)
                    close_job(mm, "oT", i)
                s = wait_load(uses, "conv_out")
                pe.wait_ge(conv_ready, l + 1)
                for i in range(4):
                    by_feature(l, "ya", i, z, chunks(s, 4, D_MODEL), i * 2 * P)
                s = wait_load(uses, "attn_out")
                wait_stages(l, "oT")
                for i in range(4):
                    by_feature(l, "yb", i, oT, chunks(s, 4, D_MODEL), i * 2 * P)
                pe.wait_ge(y_ready, l * 4 + 4)
                for i in range(4):
                    s = wait_load(uses, f"mix{i // 2}")
                    by_token(l, "mix", i, i % 2, yT, chunks(s, KC, BANK), BANK)
                for i in range(4):
                    s = wait_load(uses, f"xk{i // 2}")
                    by_feature(l, "xk", i, memT, chunks(s, KC, BANK), (i % 2) * 2 * P)
                transpose_norm(l, "xT1", 1)
                for i in range(4):
                    s = wait_load(uses, f"xq{i // 2}")
                    by_feature(l, "xq", i, XT, chunks(s, KC, BANK), (i % 2) * 2 * P, arriving="xT1")
                wait_stages(l, "xk", "xq")
                for h in range(X_HEADS):
                    w = open_job(l, "xscores", h)
                    for t in range(TT):
                        mm = accumulate(w[:, t * MEM_LEN:(t + 1) * MEM_LEN],
                                        [(xqT[:, 2 * h + c, t * P:(t + 1) * P], xkT[:, 2 * h + c, :]) for c in range(2)])
                    close_job(mm, "xscores", h)
                for i in range(4):
                    s = wait_load(uses, f"xv{i // 2}")
                    by_token(l, "xv", i, i % 2, memT, chunks(s, KC, BANK), BANK)
                for h in range(X_HEADS):
                    pe.wait_ge(xprobs_ready, l * X_HEADS + (h + 1))
                    w = open_job(l, "xpT", h)
                    for m in range(2):
                        for t in range(TT):
                            at = t * MEM_LEN + m * P
                            mm = pe.transpose(w[:, (m * TT + t) * P:(m * TT + t + 1) * P], xS[:, h, at:at + P], ident[:, :])
                    close_job(mm, "xpT", h)
                wait_stages(l, "xpT", "xv")
                for h in range(X_HEADS):
                    w = open_job(l, "xoT", h)
                    for c in range(2):
                        cols = slice(h * X_DIM + c * P, h * X_DIM + (c + 1) * P)
                        mm = accumulate(w[:, c * SEQ:(c + 1) * SEQ], [(xV[:, m, cols], xpT[:, h, m, :]) for m in range(2)])
                    close_job(mm, "xoT", h)
                wait_stages(l, "xoT")
                for i in range(4):
                    s = wait_load(uses, f"xo{i // 2}")
                    by_token(l, "xo", i, i % 2, xoT, chunks(s, KC, BANK), BANK)
                transpose_norm(l, "xT2", 2)
                s = wait_load(uses, "down_router")
                w_down_sb = chunks(s, 2, D_MODEL)
                w = open_job(l, "router")
                for t in range(TT):
                    mm = accumulate(w[:, t * P:(t + 1) * P],
                                    [(XT[:, c, t * P:(t + 1) * P],
                                      ring[:, s, 2 * D_MODEL + c * EXPERTS:2 * D_MODEL + c * EXPERTS + P])
                                     for c in range(KC)], l, "xT2")
                close_job(mm, "router")
                s = wait_load(uses, "shared")
                for i in range(2):
                    by_feature(l, "shared", i, XT, chunks(s, KC, EXPERT_DIM, i * SLOT // 2))
                pe.wait_ge(chosen_ready, l + 1)
                w = open_job(l, "place")
                both = chosen.rearrange("p t e -> p (t e)")
                pe.matmul(w[:, 0:2 * EXPERTS], earlier[:, :], both, start=True, stop=True)
                mm = pe.matmul(w[:, 2 * EXPERTS:4 * EXPERTS], ones, both, start=True, stop=True)
                close_job(mm, "place")
                wait_stages(l, "shared")
                for t in range(TT):
                    for half in range(2):
                        for c in range(2):
                            mm = pe.matmul(moe_sum[2 * t + half][:, :], sharedT[:, c, t * P:(t + 1) * P],
                                      w_down_sb[:, c, half * BANK:(half + 1) * BANK],
                                      start=(c == 0), stop=False, skip_group_check=True)
                mm.then_inc(shared_down, 1)

                def transpose_sel(b, gathers, first=False):
                    pe.wait_ge(sel_ready, gathers + l)
                    if not first:
                        pe.wait_ge(gather_ready[1], gathers - 1)
                    for t in range(TT):
                        pe.transpose(work[3][:, t * P:(t + 1) * P], sel[b][:, t, :], ident[:, :])
                    for t in range(TT):
                        mm = pe.matmul(work[3][:, SEQ:SEQ + 2], sel[b][:, t, :], gpair[b][:, t, :],
                                       start=(t == 0), stop=(t == TT - 1))
                    mm.then_inc(selT_filled, 1)

                def gather(b, half):
                    w = work[0] if half == 0 else work[3]
                    for c in range(4):
                        for t in range(TT):
                            mm = pe.matmul(w[:, c * P:(c + 1) * P], X[:, t, 4 * half + c::KC], sel[b][:, t, :],
                                           start=(t == 0), stop=(t == TT - 1))
                    mm.then_inc(gather_filled[half], 1)

                for b in range(WORK):
                    last = SETUP_USES + max(n for n in range(n_jobs) if n % WORK == b) // WORK + 1
                    if last > seen.get(b, -1):
                        pe.wait_ge(taken[b], l * BANK_USES[b] + last)
                        seen[b] = last
                pe.wait_ge(ln_applied, l * 3 + 3)
                before = pe.snap(base * 2 + l)
                transpose_sel(0, before + 1, first=True)
                gather(0, 0)
                pe.wait_ge(selT_ready, before + 1)
                gather(0, 1)

                def scatter(b, pair):
                    for half in range(2):
                        pe.wait_ge(hi_ready[half], pair)
                        pe.wait_ge(lo_ready[half], pair)
                        cols = slice(half * BANK, (half + 1) * BANK)
                        for t in range(TT):
                            for part in (out_hi, out_lo):
                                mm = pe.matmul(moe_sum[2 * t + half][:, :], selT[:, b, t * P:(t + 1) * P],
                                               part[:, cols], start=False, stop=False, skip_group_check=True)
                    mm.then_inc(scattered, 1)

                def expert_body(body, first=False):
                    loaded = pe.snap((body + (l + 1) * DENSE_USES) * 32)
                    pairs = pe.snap(body * 2)
                    gathers = pe.snap(pairs + l)
                    for j in range(2):
                        pe.wait_ge(gather_ready[0], gathers + (j + 1))
                        if first and j == 0:
                            pe.wait_ge(ahead_loaded, l * 64 + 64)
                        else:
                            for e in range(2):
                                pe.wait_ge(slot_loaded[3 * j + e], loaded + 32)
                        for c in range(KC):
                            if c == KC // 2:
                                pe.wait_ge(gather_ready[1], gathers + (j + 1))
                            for e in range(2):
                                src = ahead if first and j == 0 else ring[:, 3 * j:3 * j + 2, :]
                                wgu = src[:, e, :].rearrange("p (w k n) -> p w k n", w=2, k=KC)
                                mm = pe.matmul(work[0][e * SLOTS:(e + 1) * SLOTS, :],
                                               xg[j][:, c, e * SLOTS:(e + 1) * SLOTS], wgu[:, :, c, :],
                                               start=(c == 0), stop=(c == KC - 1))
                        mm.then_inc(gate_up_done, 1)
                        if not (first and j == 0):
                            scatter(1 - j, pairs + j)
                        transpose_sel(1 - j, gathers + (j + 2))
                        pe.wait_ge(hid_ready, pairs + (j + 1))
                        for c in range(2):
                            mm = pe.transpose(work[1][:, c * P:(c + 1) * P], hid[:, c * P:(c + 1) * P], ident[:, :])
                        mm.then_inc(hidT_filled, 1)
                        gather(1 - j, 0)
                        pe.wait_ge(hidT_ready, pairs + (j + 1))
                        pe.wait_ge(slot_loaded[3 * j + 2], loaded + 32)
                        for half in range(2):
                            w = work[2 - half]
                            for c in range(2):
                                for e in range(2):
                                    wd = chunks(3 * j + 2, 2, D_MODEL, e * SLOT // 2)
                                    mm = pe.matmul(w[e * SLOTS:(e + 1) * SLOTS, :],
                                                   hidT[:, c, e * SLOTS:(e + 1) * SLOTS],
                                                   wd[:, c, half * BANK:(half + 1) * BANK],
                                                   start=(c == 0), stop=(c == 1))
                            mm.then_inc(down_filled[half], 1)
                        pe.wait_ge(selT_ready, gathers + (j + 2))
                        gather(1 - j, 1)

                expert_body(base, first=True)
                pe.reg_mov(more, 1)
                pe.reg_mov(start, 1)
                with pe.Fori(0, more) as r:
                    with pe.Fori(start, BODIES) as i:
                        expert_body(pe.snap(base + r * BODIES + i))
                    pe.reg_mov(start, 0)
                    alone(pe, routing_ready, l + 1)
                    pe.reg_load(more, rounds[0:1, bass.ds(l, 1)])
                done = pe.value_load(bodies[0:1, bass.ds(l + 1, 1)], min_val=0, max_val=4 * BODIES * DEPTH)
                scatter(1, done * 2)
                for half in range(2):
                    pe.wait_ge(gather_ready[half], done * 2 + (l + 1))

        @block.scalar
        def _(act):
            step, tell, take, settle, restart = ordered(act, act_order)

            act.dma_start(pos_i[:, :], positions.rearrange("o (t p) -> p (o t)", p=P),
                           allow_slow_non_contiguous=True).then_inc(small_loaded, 16)
            for at, w in ((PAR_Q, q_norm), (PAR_KV, kv_norm),
                               (PAR_CONV, w_conv.rearrange("l w o d -> l (w o d)"))):
                v = w.rearrange("l (c p) -> l p c", p=P)
                for n in range(DEPTH):
                    act.dma_start(par_all[:, n, at:at + v.shape[2]], v[n],
                                   allow_slow_non_contiguous=True).then_inc(small_loaded, 16)

            act.wait_ge(angles_ready, 1)
            act.activation(sin[:, :, :], ang[:, 3, :].rearrange("p (t f) -> p t f", t=TT), ACT.Sin)
            act.activation(cos[:, :, :], ang[:, 3, :].rearrange("p (t f) -> p t f", t=TT), ACT.Sin,
                           scale=0.5).then_inc(sines_ready, 1)

            def norm_transposed(l, stage, which):
                for i in (0, 2):
                    w = wait_filled(act, l, stage, i)
                    for c in range(2):
                        k = PAR_LN + 2 * which * KC + 2 * i + c
                        ins = act.activation(XT[:, 2 * i + c, :], w[:, c * SEQ:(c + 1) * SEQ], ACT.Identity,
                                             scale=par[:, k:k + 1], bias=par[:, k + KC:k + KC + 1])
                        if c == 0:
                            step(ins)
                    take(ins, l, stage, i)

            def normalize(l, which):
                for t in range(TT):
                    act.wait_ge(ln_shift_ready, l * 6 + (2 * which + t + 1))
                    act.activation(XN[:, t, 0:BANK], X[:, t, 0:BANK], ACT.Identity, scale=ln_rstd[:, t:t + 1],
                                   bias=ln_shift[:, t:t + 1]).then_inc(norm_ready[0], 1)

            more = act.alloc_register("act_rounds")
            act.wait_ge(consts_ready, 1)
            with act.Fori(0, DEPTH) as l:
                base = act.value_load(bodies[0:1, bass.ds(l, 1)], min_val=0, max_val=4 * BODIES * DEPTH)
                norm_transposed(l, "xT0", 2)
                junk = view(9 * K, Q_RANK)
                for i, (stage, n) in enumerate((("cq", Q_RANK), ("cq", Q_RANK), ("ckv", KV_RANK), ("ckv", KV_RANK))):
                    w = wait_filled(act, l, stage, i % 2)
                    settle()
                    tell(act.activation(junk[:, 0:n], w[:, 0:n], ACT.Square, scale=n ** -0.5,
                                        accum_out=sumsq[:, i:i + 1]),
                         squares_ready, l * 4 + i + 1)
                for i in range(2):
                    w = wait_filled(act, l, "c", i)
                    take(act.copy(c_sb[:, 2 * i:2 * i + 2, :], w[:, :].rearrange("p (m t) -> p m t", m=2)), l, "c", i)
                for i in range(2):
                    w = wait_filled(act, l, "b", i)
                    take(act.copy(b_sb[:, 2 * i:2 * i + 2, :], w[:, :].rearrange("p (m t) -> p m t", m=2)), l, "b", i)
                for i in range(4):
                    w = wait_filled(act, l, "uq", i)
                    take(act.copy(q_cat[:, i // 2, 4 * (i % 2):4 * (i % 2) + 4, :],
                                  w[:, 0:Q_RANK].rearrange("p (h d) -> p h d", h=4)), l, "uq", i)
                for t in range(TT):
                    w = wait_filled(act, l, "uk", t)
                    take(act.copy(k_cat[:, t, :, 0:NOPE], w[:, :].rearrange("p (h d) -> p h d", h=HEADS)), l, "uk", t)
                for t in range(TT):
                    w = wait_filled(act, l, "uv", t)
                    take(act.copy(V[:, t, :], w[:, :]), l, "uv", t)
                for i in range(2):
                    w = wait_filled(act, l, "ga0", i)
                    take(act.activation(sgA[:, 2 * i:2 * i + 2, :], w[:, :].rearrange("p (m t) -> p m t", m=2),
                                        ACT.Sigmoid), l, "ga0", i)
                for i in range(0, 8, 2):
                    t, g = i // 2 % 2, i // 4
                    w = wait_filled(act, l, "qkT", i)
                    take(act.copy(qT[0:QK, 4 * g:4 * g + 4, t * P:(t + 1) * P],
                                  w[0:QK, :].rearrange("p (h t) -> p h t", h=4)), l, "qkT", i)

                def exps(g):
                    act.wait_ge(max_ready, l * 2 + (g + 1))
                    for h in range(4 * g, 4 * g + 4):
                        for t, cols in ((0, slice(0, P)), (1, slice(P, 3 * P))):
                            ins = act.activation(S[:, h, cols], S[:, h, cols], ACT.Exp, scale=MLA_SCALE,
                                                 bias=row_max[:, h, t:t + 1], accum_out=row_sum[:, h, t:t + 1])
                    ins.then_inc(exp_ready, 1)

                exps(0)
                exps(1)
                for i in range(2):
                    w = wait_filled(act, l, "ga1", i)
                    take(act.activation(sgA[:, 4 + 2 * i:6 + 2 * i, :], w[:, :].rearrange("p (m t) -> p m t", m=2),
                                        ACT.Sigmoid), l, "ga1", i)
                act.wait_ge(conv_ready, l + 1)
                for i in range(4):
                    w = wait_filled(act, l, "gb", i)
                    take(act.activation(sgB[:, 2 * i:2 * i + 2, :], w[:, :].rearrange("p (m t) -> p m t", m=2),
                                        ACT.Sigmoid), l, "gb", i)
                for h in range(0, HEADS, 2):
                    w = wait_filled(act, l, "pT", h)
                    take(act.copy(pT[:, h, :], w[:, 0:3 * P]), l, "pT", h)
                w = wait_filled(act, l, "oT", 0)
                take(act.copy(oT[:, 0:2, :], w[:, :].rearrange("p (a t) -> p a t", a=2)), l, "oT", 0)
                for i in range(4):
                    w = wait_filled(act, l, "xk", i)
                    take(act.copy(xkT[:, 2 * i:2 * i + 2, :], w[:, :].rearrange("p (m t) -> p m t", m=2)), l, "xk", i)
                normalize(l, 0)
                norm_transposed(l, "xT1", 0)
                for i in range(4):
                    w = wait_filled(act, l, "xq", i)
                    take(act.copy(xqT[:, 2 * i:2 * i + 2, :], w[:, :].rearrange("p (m t) -> p m t", m=2)), l, "xq", i)
                for h in range(X_HEADS):
                    act.wait_ge(xmax_ready, l * X_HEADS + (h + 1))
                    w = wait_filled(act, l, "xscores", h)
                    for t in range(TT):
                        cols = slice(t * MEM_LEN, (t + 1) * MEM_LEN)
                        ins = act.activation(xS[:, h, cols], w[:, cols], ACT.Exp, scale=X_SCALE,
                                             bias=row_max[:, h, t:t + 1], accum_out=row_sum[:, h, t:t + 1])
                    take(ins, l, "xscores", h)
                for i in range(4):
                    w = wait_filled(act, l, "xv", i)
                    take(act.copy(xV[:, i % 2, (i // 2) * BANK:(i // 2 + 1) * BANK], w[:, :]), l, "xv", i)
                for h in range(0, X_HEADS, 2):
                    w = wait_filled(act, l, "xpT", h)
                    take(act.copy(xpT[:, h, :, :], w[:, :].rearrange("p (m t) -> p m t", m=2)), l, "xpT", h)
                for h in range(0, X_HEADS, 2):
                    w = wait_filled(act, l, "xoT", h)
                    take(act.copy(xoT[:, 2 * h:2 * h + 2, :], w[:, :].rearrange("p (m t) -> p m t", m=2)), l, "xoT", h)
                normalize(l, 1)
                norm_transposed(l, "xT2", 1)
                w = wait_filled(act, l, "router")
                take(act.activation(score, w[:, 0:TT * P].rearrange("p (t e) -> p t e", t=TT)[:, :, 0:EXPERTS], ACT.Sigmoid),
                     l, "router")
                w = wait_filled(act, l, "shared", 0)
                take(act.activation(shared_act, w[:, :].rearrange("p (m t) -> p m t", m=2), ACT.Silu),
                     l, "shared", 0)

                def take_sel(b, gathers):
                    act.wait_ge(selT_filled, gathers)
                    act.copy(selT[:, b, :], work[3][:, 0:SEQ])
                    act.copy(slot_gate[0:SLOTS, b:b + 1], work[3][0:SLOTS, SEQ:SEQ + 1])
                    act.copy(slot_gate[SLOTS:P, b:b + 1], work[3][SLOTS:P, SEQ + 1:SEQ + 2]).then_inc(selT_ready, 1)

                def take_gather(b, gathers):
                    act.wait_ge(gather_filled[0], gathers)
                    act.copy(xg[b][:, 0:4, :], work[0][:, :].rearrange("p (c s) -> p c s", c=4)
                             ).then_inc(gather_ready[0], 1)

                before = act.snap(base * 2 + l)
                take_sel(0, before + 1)
                take_gather(0, before + 1)
                act.reg_mov(more, 1)
                with act.Fori(0, more) as r:
                    with act.Fori(0, BODIES) as i:
                        pairs = act.snap((base + r * BODIES + i) * 2)
                        gathers = act.snap(pairs + l)
                        for j in range(2):
                            act.wait_ge(gate_up_done, pairs + (j + 2))
                            act.activation(act_gate, work[0][:, 0:EXPERT_DIM], ACT.Silu).then_inc(silu_ready, 1)
                            take_sel(1 - j, gathers + (j + 2))
                            take_gather(1 - j, gathers + (j + 2))
                            for half in range(2):
                                act.wait_ge(down_filled[half], pairs + (j + 1 + half))
                                act.copy(out_hi[:, half * BANK:(half + 1) * BANK], work[2 - half][:, :]
                                         ).then_inc(hi_ready[half], 1)
                    alone(act, routing_ready, l + 1)
                    act.reg_load(more, rounds[0:1, bass.ds(l, 1)])
                normalize(l, 2)
                restart()

        @block.vector
        def _(dve):
            step, tell, take, settle, restart = ordered(dve, dve_order)

            def then(ins):
                step(ins)
                settle()

            for b in range(WORK):
                dve.wait_ge(filled[b], 1)
                dve.tensor_copy(memT[:, 2 * b:2 * b + 2, :], work[b][:, :].rearrange("p (c t) -> p c t", c=2)
                                ).then_inc(taken[b], 1)
            step(dve.memset(par[:, PAR_LN + 4 * KC:PAR_LN + 5 * KC], 1.0))
            step(dve.memset(par[:, PAR_LN + 5 * KC:PAR_LN + 6 * KC], 0.0))
            dve.wait_ge(x_loaded, 16)
            for t in range(TT):
                for half in range(2):
                    cols = slice(half * BANK, (half + 1) * BANK)
                    dve.tensor_copy(XN[:, t, cols], X[:, t, cols]).then_inc(norm_ready[half], 1)
            dve.wait_ge(small_loaded, SMALL_LOADS * 16)
            dve.wait_ge(consts_ready, 2)
            then(dve.tensor_copy(pos_f, pos_i[:, :]))
            a3 = [ang[:, i, :].rearrange("p (t f) -> p t f", t=TT) for i in range(4)]
            then(dve.tensor_tensor(a3[0], pos_f.unsqueeze(2).to_broadcast([P, TT, HALF_ROPE]),
                                   inv_freq[:, :].unsqueeze(1).to_broadcast([P, TT, HALF_ROPE]), ALU.mult))
            magic = 1.5 * 2.0 ** 23
            then(dve.tensor_scalar(ang[:, 1, :], ang[:, 0, :], 1.0 / (2.0 * np.pi), magic, ALU.mult, ALU.add))
            then(dve.tensor_scalar(ang[:, 1, :], ang[:, 1, :], -magic, None, ALU.add))
            c1 = 6.28125
            c2 = float(np.float32(np.floor((2 * np.pi - c1) * 2.0 ** 19) / 2.0 ** 19))
            c3 = float(np.float32(2 * np.pi - c1 - c2))
            for src, dst, c in ((0, 2, c1), (2, 4, c2), (4, 5, c3)):
                then(dve.scalar_tensor_tensor(out=ang[:, dst, :], in0=ang[:, 1, :], scalar=-c, in1=ang[:, src, :],
                                              op0=ALU.mult, op1=ALU.add))
            dve.tensor_scalar(ang[:, 3, :], ang[:, 5, :], 3.1415925, -3.1415925, ALU.min, ALU.max
                              ).then_inc(angles_ready, 1)
            dve.wait_ge(sines_ready, 1)
            then(dve.tensor_tensor(cos[:, :, :], cos[:, :, :], cos[:, :, :], ALU.mult))
            then(dve.tensor_scalar(cos[:, :, :], cos[:, :, :], -2.0, 1.0, ALU.mult, ALU.add))
            restart()

            def add_and_normalize(l, stage, which):
                dve.wait_ge(ln_applied, l * 3 + which + 1)
                for i in range(4):
                    t, half = (i % 2, i // 2) if stage else (i // 2, i % 2)
                    cols = slice(half * BANK, (half + 1) * BANK)
                    w = wait_filled(dve, l, stage, i) if stage else moe_sum[2 * t + half]
                    ins = dve.scalar_tensor_tensor(out=X[:, t, cols], in0=X[:, t, cols], scalar=ALPHA, in1=w[:, :],
                                                   op0=ALU.mult, op1=ALU.add)
                    if stage:
                        take(ins, l, stage, i)
                    else:
                        step(ins)
                    settle()
                    step(dve.bn_stats(stats[:, t, 6 * half:6 * half + 6], X[:, t, cols]))
                    if half == 1:
                        settle()
                        tell(dve.bn_aggr(moments[:, 2 * t:2 * t + 2], stats[:, t, :]), moments_ready,
                             l * 6 + (2 * which + t + 1))
                def centre(t):
                    return dve.scalar_tensor_tensor(out=centred[:, t, :], in0=X[:, t, :],
                                                    scalar=moments[:, 2 * t:2 * t + 1], in1=gb[:, 0, :],
                                                    op0=ALU.subtract, op1=ALU.mult)

                if which == 2:
                    dve.wait_ge(ln_loaded, (l * 3 + 3) * 32)
                    settle()
                    step(centre(0))
                for t in range(TT):
                    dve.wait_ge(ln_rstd_ready, l * 6 + (2 * which + t + 1))
                    tell(dve.tensor_scalar(XN[:, t, BANK:], X[:, t, BANK:], moments[:, 2 * t:2 * t + 1],
                                           ln_rstd[:, t:t + 1], ALU.subtract, ALU.mult),
                         norm_ready[1], l * 6 + (2 * which + t + 3))
                if which == 2:
                    for t in range(TT):
                        if t == 1:
                            step(centre(1))
                        dve.wait_ge(norm_ready[0], l * 6 + (t + 7))
                        settle()
                        tell(dve.scalar_tensor_tensor(out=X[:, t, :], in0=centred[:, t, :],
                                                      scalar=ln_rstd[:, t:t + 1], in1=gb[:, 1, :],
                                                      op0=ALU.mult, op1=ALU.add),
                             (layer_done if t == 0 else ln_applied), (l + 1 if t == 0 else l * 3 + 4))

            def norm_transposed(l, stage, which):
                for i in (1, 3):
                    w = wait_filled(dve, l, stage, i)
                    for c in range(2):
                        k = PAR_LN + 2 * which * KC + 2 * i + c
                        ins = dve.tensor_scalar(XT[:, 2 * i + c, :], w[:, c * SEQ:(c + 1) * SEQ],
                                                par[:, k:k + 1], par[:, k + KC:k + KC + 1], ALU.mult, ALU.add)
                        if c == 0:
                            step(ins)
                    take(ins, l, stage, i)

            more = dve.alloc_register("dve_rounds")
            with dve.Fori(0, DEPTH) as l:
                base = dve.value_load(bodies[0:1, bass.ds(l, 1)], min_val=0, max_val=4 * BODIES * DEPTH)
                then(dve.tensor_copy(par[:, 0:PAR_LN], par_all[:, bass.ds(l, 1), 0:PAR_LN].rearrange("p o n -> p (o n)")))
                norm_transposed(l, "xT0", 2)
                for i in range(4):
                    stage, t = ("cq", "ckv")[i // 2], i % 2
                    n = (Q_RANK, KV_RANK)[i // 2]
                    dve.wait_ge(rstd_ready, l * 4 + (i + 1))
                    w = work[job(stage, t)[0]]
                    if i >= 2:
                        step(dve.tensor_copy(kr[:, t, :], w[:, KV_RANK:KV_RANK + ROPE]))
                    take(dve.tensor_scalar((cqn, ckvn)[i // 2][:, t, :], w[:, 0:n], rstd[:, i:i + 1], None,
                                                ALU.mult), l, stage, t)
                step(dve.memset(u_pad[:, :, 0:2], 0.0))
                for i in range(2):
                    wait_taken(dve, l, "c", 1, i)
                    w = wait_filled(dve, l, "h", i)
                    take(dve.tensor_tensor(u_pad[:, 2 * i:2 * i + 2, 2:], w[:, :].rearrange("p (m t) -> p m t", m=2),
                                                c_sb[:, 2 * i:2 * i + 2, :], ALU.mult), l, "h", i)
                settle()
                for i, chunks_of in enumerate(([(cqT, 0), (cqT, 1)], [(cqT, 2)], [(ckvT, 0), (ckvT, 1)])):
                    w = wait_filled(dve, l, "rankT", i)
                    for j, (dst, c) in enumerate(chunks_of):
                        g = (PAR_Q if dst is cqT else PAR_KV) + c
                        ins = dve.tensor_scalar(dst[:, c, :], w[:, j * SEQ:(j + 1) * SEQ], par[:, g:g + 1], None,
                                                ALU.mult)
                    take(ins, l, "rankT", i)
                for k in range(CONV_WIDTH):
                    for c in range(CONV_DIM // P):
                        g = PAR_CONV + k * (CONV_DIM // P) + c
                        if k == 0:
                            step(dve.tensor_scalar(z[:, c, :], u_pad[:, c, 0:SEQ], par[:, g:g + 1], None, ALU.mult))
                        else:
                            step(dve.scalar_tensor_tensor(out=z[:, c, :], in0=u_pad[:, c, k:k + SEQ], scalar=par[:, g:g + 1],
                                                          in1=z[:, c, :], op0=ALU.mult, op1=ALU.add))
                    settle()
                wait_taken(dve, l, "b")
                tell(dve.tensor_tensor(z, z, b_sb, ALU.mult), conv_ready, l + 1)
                wait_taken(dve, l, "uq")

                def rotate(x1, x2, o1, o2, cs, sn, buf):
                    a, b, c, d = buf
                    step(dve.tensor_tensor(a, x1, cs, ALU.mult))
                    step(dve.tensor_tensor(b, x2, sn, ALU.mult))
                    step(dve.tensor_tensor(c, x2, cs, ALU.mult))
                    step(dve.tensor_tensor(d, x1, sn, ALU.mult))
                    settle()
                    step(dve.tensor_tensor(o1, a, b, ALU.subtract))
                    step(dve.tensor_tensor(o2, c, d, ALU.add))

                for t in range(TT):
                    shape = [P, HEADS, HALF_ROPE]
                    cs = cos[:, t:t + 1, :].to_broadcast(shape)
                    sn = sin[:, t:t + 1, :].to_broadcast(shape)
                    buf = [rope_t[:, i, t * HEADS * HALF_ROPE:(t + 1) * HEADS * HALF_ROPE]
                           .rearrange("p (h f) -> p h f", h=HEADS) for i in range(4)]
                    x1, x2 = q_cat[:, t, :, NOPE:NOPE + HALF_ROPE], q_cat[:, t, :, NOPE + HALF_ROPE:QK]
                    rotate(x1, x2, x1, x2, cs, sn, buf)
                settle()
                buf = [rope_t[:, i, 0:TT * HALF_ROPE].rearrange("p (t f) -> p t f", t=TT) for i in range(4)]
                x1, x2 = kr[:, :, 0:HALF_ROPE], kr[:, :, HALF_ROPE:ROPE]
                rotate(x1, x2, x1, x2, cos[:, :, :], sin[:, :, :], buf)
                settle()
                wait_taken(dve, l, "uk")
                for t in range(TT):
                    ins = dve.tensor_copy(k_cat[:, t, :, NOPE:QK], kr[:, t:t + 1, :].to_broadcast([P, HEADS, ROPE]))
                    if t == 0:
                        step(ins)
                    else:
                        tell(ins, qk_ready, l + 1)
                for i in range(1, 8, 2):
                    t, g = i // 2 % 2, i // 4
                    w = wait_filled(dve, l, "qkT", i)
                    take(dve.tensor_copy(kT[0:QK, 4 * g:4 * g + 4, t * P:(t + 1) * P],
                                         w[0:QK, :].rearrange("p (h t) -> p h t", h=4)), l, "qkT", i)
                wait_taken(dve, l, "xT0")
                dve.wait_ge(norm_loaded, NORM_LOADS * 16)
                step(dve.tensor_copy(par[:, PAR_LN:], par_all[:, bass.ds(l, 1), PAR_LN:].rearrange("p o n -> p (o n)")))
                def maxima(g):
                    for h in range(4 * g, 4 * g + 4):
                        w = wait_filled(dve, l, "scores", h)
                        take(dve.tensor_tensor(S[:, h, :], w[:, 0:3 * P], mask[:, :], ALU.add), l, "scores", h)
                    settle()
                    hs = slice(4 * g, 4 * g + 4)
                    step(dve.tensor_reduce(row_max[:, hs, 0], S[:, hs, 0:P], AX_X, ALU.max))
                    step(dve.tensor_reduce(row_max[:, hs, 1], S[:, hs, P:3 * P], AX_X, ALU.max))
                    settle()
                    tell(dve.tensor_scalar(row_max[:, hs, :], row_max[:, hs, :], -MLA_SCALE, None, ALU.mult),
                         max_ready, l * 2 + (g + 1))

                def normalize(g):
                    hs = slice(4 * g, 4 * g + 4)
                    dve.wait_ge(exp_ready, l * 2 + (g + 1))
                    then(dve.reciprocal(row_sum[:, hs, :], row_sum[:, hs, :]))
                    step(dve.tensor_tensor(S[:, hs, 0:P], S[:, hs, 0:P],
                                           row_sum[:, hs, 0:1].to_broadcast([P, 4, P]), ALU.mult))
                    tell(dve.tensor_tensor(S[:, hs, P:3 * P], S[:, hs, P:3 * P],
                                           row_sum[:, hs, 1:2].to_broadcast([P, 4, 2 * P]), ALU.mult),
                         probs_ready, l * 2 + (g + 1))

                maxima(0)
                maxima(1)
                normalize(0)
                normalize(1)
                for h in range(1, HEADS, 2):
                    w = wait_filled(dve, l, "pT", h)
                    take(dve.tensor_copy(pT[:, h, :], w[:, 0:3 * P]), l, "pT", h)
                w = wait_filled(dve, l, "oT", 1)
                take(dve.tensor_copy(oT[:, 2:4, :], w[:, :].rearrange("p (a t) -> p a t", a=2)), l, "oT", 1)
                wait_taken(dve, l, "ga0")
                wait_taken(dve, l, "ga1")
                for i in range(4):
                    w = wait_filled(dve, l, "ya", i)
                    cs = slice(2 * i, 2 * i + 2)
                    take(dve.tensor_tensor(yT[:, cs, :], w[:, :].rearrange("p (m t) -> p m t", m=2), sgA[:, cs, :],
                                                ALU.mult), l, "ya", i)
                wait_taken(dve, l, "gb")
                for i in range(4):
                    w = wait_filled(dve, l, "yb", i)
                    cs = slice(2 * i, 2 * i + 2)
                    take(dve.tensor_tensor(sgB[:, cs, :], w[:, :].rearrange("p (m t) -> p m t", m=2), sgB[:, cs, :],
                                                ALU.mult), l, "yb", i)
                    settle()
                    tell(dve.tensor_tensor(yT[:, cs, :], yT[:, cs, :], sgB[:, cs, :], ALU.add),
                         y_ready, l * 4 + (i + 1))
                add_and_normalize(l, "mix", 0)
                norm_transposed(l, "xT1", 0)
                for h in range(X_HEADS):
                    w = wait_filled(dve, l, "xscores", h)
                    then(dve.tensor_reduce(row_max[:, h, :], w[:, :].rearrange("p (t m) -> p t m", t=TT), AX_X, ALU.max))
                    tell(dve.tensor_scalar(row_max[:, h, :], row_max[:, h, :], -X_SCALE, None, ALU.mult),
                         xmax_ready, l * X_HEADS + (h + 1))
                for h in range(X_HEADS):
                    wait_taken(dve, l, "xscores", 1, h)
                    then(dve.reciprocal(row_sum[:, h, :], row_sum[:, h, :]))
                    xs = xS[:, h, :].rearrange("p (t m) -> p t m", t=TT)
                    tell(dve.tensor_tensor(xs, xs, row_sum[:, h, :].unsqueeze(2).to_broadcast([P, TT, MEM_LEN]),
                                           ALU.mult), xprobs_ready, l * X_HEADS + (h + 1))
                for h in range(1, X_HEADS, 2):
                    w = wait_filled(dve, l, "xpT", h)
                    take(dve.tensor_copy(xpT[:, h, :, :], w[:, :].rearrange("p (m t) -> p m t", m=2)), l, "xpT", h)
                for h in range(1, X_HEADS, 2):
                    w = wait_filled(dve, l, "xoT", h)
                    take(dve.tensor_copy(xoT[:, 2 * h:2 * h + 2, :], w[:, :].rearrange("p (m t) -> p m t", m=2)), l, "xoT", h)
                add_and_normalize(l, "xo", 1)
                norm_transposed(l, "xT2", 1)
                step(dve.memset(ones, 1.0))
                step(dve.tensor_scalar(before_group, iota[:, 0:GROUPS].unsqueeze(1).to_broadcast([P, GROUPS, GROUPS]),
                                       1.0, None, ALU.mult))
                settle()
                step(dve.tensor_tensor(before_group, before_group,
                                       iota[:, 0:GROUPS].unsqueeze(2).to_broadcast([P, GROUPS, GROUPS]), ALU.is_lt))
                wait_taken(dve, l, "router")
                bias = par[:, PAR_BIAS:PAR_BIAS + EXPERTS].unsqueeze(1).to_broadcast([P, TT, EXPERTS])
                then(dve.tensor_tensor(biased, score, bias, ALU.add))
                for t in range(TT):
                    for g in range(GROUPS):
                        step(dve.max(top2[:, t * GROUPS + g, :], biased[:, t, g * 8:(g + 1) * 8]))
                settle()
                then(dve.tensor_tensor(group_score, top2[:, :, 0], top2[:, :, 1], ALU.add))
                for t in range(TT):
                    gs = group_score[:, t * GROUPS:(t + 1) * GROUPS]
                    other = gs.unsqueeze(1).to_broadcast([P, GROUPS, GROUPS])
                    own = gs.unsqueeze(2).to_broadcast([P, GROUPS, GROUPS])
                    rows = slice(t * GROUPS, (t + 1) * GROUPS)
                    step(dve.tensor_tensor(cmp_a[:, rows, :], other, own, ALU.is_gt))
                    then(dve.tensor_tensor(cmp_b[:, rows, :], other, own, ALU.is_equal))
                    then(dve.tensor_tensor(cmp_b[:, rows, :], cmp_b[:, rows, :], before_group, ALU.mult))
                    then(dve.tensor_tensor(cmp_a[:, rows, :], cmp_a[:, rows, :], cmp_b[:, rows, :], ALU.add))
                then(dve.tensor_reduce(group_rank, cmp_a, AX_X, ALU.add))
                then(dve.tensor_scalar(penalty[:, :], group_rank, TOP_GROUPS - 0.5, MASKED, ALU.is_gt, ALU.mult))
                then(dve.tensor_tensor(masked.rearrange("p t (g e) -> p (t g) e", g=GROUPS),
                                       biased.rearrange("p t (g e) -> p (t g) e", g=GROUPS),
                                       penalty[:, :].unsqueeze(2).to_broadcast([P, TT * GROUPS, EXPERTS // GROUPS]),
                                       ALU.add))
                for t in range(TT):
                    then(dve.max(top8[:, t, :], masked[:, t, :]))
                    step(dve.match_replace(marked[:, t, :], top8[:, t, :], masked[:, t, :], TAKEN))
                settle()
                tell(dve.tensor_scalar(chosen, marked, TAKEN, None, ALU.is_equal), chosen_ready, l + 1)
                settle()
                wait_taken(dve, l, "shared", 1)
                w = wait_filled(dve, l, "shared", 1)
                take(dve.tensor_tensor(sharedT, shared_act, w[:, :].rearrange("p (m t) -> p m t", m=2), ALU.mult),
                     l, "shared", 1)
                then(dve.tensor_tensor(weight, score, chosen, ALU.mult))
                then(dve.tensor_reduce(gate_sum[:, :], weight, AX_X, ALU.add))
                then(dve.reciprocal(gate_sum[:, :], gate_sum[:, :]))
                then(dve.tensor_scalar(gate_sum[:, :], gate_sum[:, :], ROUTE_SCALE, None, ALU.mult))
                then(dve.tensor_tensor(gates[:, :, 0:EXPERTS], weight,
                                       gate_sum[:, :].unsqueeze(2).to_broadcast([P, TT, EXPERTS]), ALU.mult))
                step(dve.tensor_copy(gates[:, :, EXPERTS:PADDED], gates[:, :, 0:4]))
                w = wait_filled(dve, l, "place")
                then(dve.tensor_scalar(pos[:, :, 0:EXPERTS], chosen, -FAR, FAR, ALU.mult, ALU.add))
                step(dve.tensor_tensor(pos[:, :, 0:EXPERTS], pos[:, :, 0:EXPERTS],
                                       w[:, 0:2 * EXPERTS].rearrange("p (t e) -> p t e", t=TT), ALU.add))
                then(dve.tensor_copy(marked, w[:, 2 * EXPERTS:4 * EXPERTS].rearrange("p (t e) -> p t e", t=TT)))
                take(dve.tensor_tensor(weight[:, 0, :], marked[:, 0, :], w[:, 3 * EXPERTS:4 * EXPERTS], ALU.add), l, "place")
                settle()
                step(dve.tensor_tensor(pos[:, 1, 0:EXPERTS], pos[:, 1, 0:EXPERTS], marked[:, 0, :], ALU.add))
                step(dve.tensor_reduce(busiest[:, 0:1], weight[:, 0, :], AX_X, ALU.max))
                settle()
                step(dve.tensor_scalar(pos[:, :, EXPERTS:PADDED], pos[:, :, 0:4], -float(SLOTS), None, ALU.add))
                then(dve.tensor_scalar(busiest[:, 1:2], busiest[:, 0:1], float(SLOTS), 1.0, ALU.is_gt, ALU.add))
                for n in range(2, SEQ // SLOTS):
                    then(dve.tensor_scalar(busiest[:, 2:3], busiest[:, 0:1], float(n * SLOTS), None, ALU.is_gt))
                    then(dve.tensor_tensor(busiest[:, 1:2], busiest[:, 1:2], busiest[:, 2:3], ALU.add))
                step(dve.tensor_copy(rounds[:, bass.ds(l, 1)], busiest[0:1, 1:2]))
                then(dve.tensor_copy(bodies_f[:, 0:1], bodies[:, bass.ds(l, 1)]))
                then(dve.scalar_tensor_tensor(out=bodies_f[:, 1:2], in0=busiest[0:1, 1:2], scalar=float(BODIES),
                                              in1=bodies_f[:, 0:1], op0=ALU.mult, op1=ALU.add))
                tell(dve.tensor_copy(bodies[:, bass.ds(l + 1, 1)], bodies_f[:, 1:2]), routing_ready, l + 1)

                def build_sel(b, first):
                    dve.tensor_tensor(
                        sel[b].rearrange("p t (e s) -> p t e s", e=2),
                        pos[:, :, first].unsqueeze(3).to_broadcast([P, TT, 2, SLOTS]),
                        iota[:, :].unsqueeze(1).unsqueeze(1).to_broadcast([P, TT, 2, SLOTS]), ALU.is_equal)
                    dve.tensor_copy(gpair[b], gates[:, :, first]).then_inc(sel_ready, 1)

                def take_gather(b, gathers):
                    dve.wait_ge(gather_filled[1], gathers)
                    dve.tensor_copy(xg[b][:, 4:8, :], work[3][:, :].rearrange("p (c s) -> p c s", c=4)
                                    ).then_inc(gather_ready[1], 1)

                settle()
                for j in range(2):
                    build_sel(j, slice(2 * j, 2 * j + 2))
                take_gather(0, base * 2 + (l + 1))
                restart()
                dve.reg_mov(more, 1)
                with dve.Fori(0, more) as r:
                    with dve.Fori(0, BODIES) as i:
                        pairs = dve.snap((base + r * BODIES + i) * 2)
                        gathers = dve.snap(pairs + l)
                        for j in range(2):
                            dve.wait_ge(silu_ready, pairs + (j + 1))
                            dve.scalar_tensor_tensor(out=hid, in0=act_gate, scalar=slot_gate[:, j:j + 1],
                                                     in1=work[0][:, EXPERT_DIM:2 * EXPERT_DIM],
                                                     op0=ALU.mult, op1=ALU.mult).then_inc(hid_ready, 1)
                            dve.wait_ge(hidT_filled, pairs + (j + 1))
                            dve.tensor_copy(hidT, work[1][:, 0:2 * P].rearrange("p (c s) -> p c s", c=2)
                                            ).then_inc(hidT_ready, 1)
                            build_sel(j, bass.ds(i * 4 + (2 * j + 4), 2))
                            for half in range(2):
                                cols = slice(half * BANK, (half + 1) * BANK)
                                dve.wait_ge(hi_ready[half], pairs + (j + 1))
                                dve.tensor_tensor(out_lo[:, cols], work[2 - half][:, :], out_hi[:, cols].bitcast(F32),
                                                  ALU.subtract).then_inc(lo_ready[half], 1)
                            take_gather(1 - j, gathers + (j + 2))
                    dve.wait_ge(sel_ready, (base + (r + 1) * BODIES) * 2 + (l * 2 + 2))
                    then(dve.tensor_scalar(pos, pos, -float(SLOTS), None, ALU.add))
                    restart()
                    alone(dve, routing_ready, l + 1)
                    dve.reg_load(more, rounds[0:1, bass.ds(l, 1)])
                done = dve.value_load(bodies[0:1, bass.ds(l + 1, 1)], min_val=0, max_val=4 * BODIES * DEPTH)
                dve.wait_ge(scattered, done * 2)
                add_and_normalize(l, None, 2)
                restart()


_INS = ["x", "mem", "positions", "w_in", "w_conv", "w_conv_out", "q_norm", "w_uq", "kv_norm", "w_uk", "w_uv",
        "w_attn_out", "w_mix_out", "ln1_g", "ln1_b", "w_xq", "w_xk", "w_xv", "w_xo", "ln2_g", "ln2_b",
        "w_router", "router_bias", "w_gate", "w_up", "w_down", "ws_gate", "ws_up", "ws_down", "ln3_g", "ln3_b"]


def kernel(**inputs):
    import numpy as _np
    import concourse.bacc as _bacc
    from concourse import mybir as _mybir
    from concourse.bass_utils import run_bass_kernel_spmd as _run

    nc = _bacc.Bacc("TRN2", target_bir_lowering=False, num_devices=1)
    arrays, args = {}, []
    for name in _INS:
        a = _np.ascontiguousarray(inputs[name])
        arrays[f"in_{name}"] = a
        args.append(nc.dram_tensor(f"in_{name}", a.shape, _mybir.dt.from_np(a.dtype), kind="ExternalInput").ap())
    args.append(nc.dram_tensor("out_0", inputs["x"].shape, _mybir.dt.float32, kind="ExternalOutput").ap())
    build_trunk(nc, *args)
    r = _run(nc, [arrays], core_ids=[0])
    return r.results[0]["out_0"]
```
